# Optimizing a Trainium2 kernel written in Bass

```python
import math
import jax, jax.numpy as jnp
from jax import lax
import numpy as np

D_MODEL = 1024
BATCH = 1
SEQ = 1024
DEPTH = 1

CHUNK = 64
HEAD_DIM = 64
RMS_EPS = 1e-6
NEG_INF = -1e30

A_HEADS = 8
A_KV_HEADS = 2
A_GROUP = A_HEADS // A_KV_HEADS
A_WINDOW = 128
A_WIN_CHUNKS = A_WINDOW // CHUNK
A_WIDTH = A_HEADS * HEAD_DIM

B_HEADS = 4
B_VDIM = 2 * HEAD_DIM
B_WIDTH = B_HEADS * B_VDIM
B_QBLOCK = 128

MIX_WIDTH = A_WIDTH + B_WIDTH
A_Q_COLS = A_HEADS * HEAD_DIM
A_K_COLS = A_KV_HEADS * HEAD_DIM
A_V_COLS = A_KV_HEADS * HEAD_DIM
A_G_COLS = A_WIDTH
B_Q_COLS = B_HEADS * 2 * HEAD_DIM
B_K_COLS = B_HEADS * 2 * HEAD_DIM
B_V_COLS = B_WIDTH
B_G_COLS = B_WIDTH
IN_WIDTH = A_Q_COLS + A_K_COLS + A_V_COLS + A_G_COLS + B_Q_COLS + B_K_COLS + B_V_COLS + B_G_COLS

kernel_name = "hybrid_swa_sink_diffattn_alibi_sandwich"

def rmsnorm(x, g):
    xf = x.astype(jnp.float32)
    y = xf * lax.rsqrt(jnp.mean(xf * xf, axis=-1, keepdims=True) + RMS_EPS)
    return (y * g.astype(jnp.float32)).astype(x.dtype)

def alibi_slopes(n):
    return jnp.asarray(np.array([2.0 ** (-8.0 * (i + 1) / n) for i in range(n)], dtype=np.float32))

def split_projection(p):
    sizes = [A_Q_COLS, A_K_COLS, A_V_COLS, A_G_COLS, B_Q_COLS, B_K_COLS, B_V_COLS, B_G_COLS]
    offs = [0]
    for s in sizes:
        offs.append(offs[-1] + s)
    return [p[..., offs[i]:offs[i + 1]] for i in range(len(sizes))]

def sliding_window_sink_attention(q, k, v, sinks):
    bsz, t, _, _ = q.shape
    nc = t // CHUNK
    span = A_WIN_CHUNKS * CHUNK
    qb = q.reshape(bsz, nc, CHUNK, A_KV_HEADS, A_GROUP, HEAD_DIM)

    def band(a):
        ac = a.reshape(bsz, nc, CHUNK, A_KV_HEADS, HEAD_DIM)
        ap = jnp.pad(ac, ((0, 0), (A_WIN_CHUNKS - 1, 0), (0, 0), (0, 0), (0, 0)))
        return jnp.concatenate([ap[:, j:j + nc] for j in range(A_WIN_CHUNKS)], axis=2)

    kb, vb = band(k), band(v)
    scale = 1.0 / math.sqrt(HEAD_DIM)
    s = jnp.einsum('bcqkgd,bcskd->bckgqs', qb, kb).astype(jnp.float32) * scale

    chunk_idx = jnp.arange(nc)
    q_pos = chunk_idx[:, None] * CHUNK + jnp.arange(CHUNK)[None, :]
    k_pos = (chunk_idx[:, None] - (A_WIN_CHUNKS - 1)) * CHUNK + jnp.arange(span)[None, :]
    dist = jnp.abs(q_pos[:, :, None] - k_pos[:, None, :]).astype(jnp.float32)
    slopes = alibi_slopes(A_HEADS).reshape(A_KV_HEADS, A_GROUP)
    bias = -slopes[None, :, :, None, None] * dist[:, None, None, :, :]
    valid = (k_pos >= 0)[:, None, None, None, :]
    s = jnp.where(valid[None], s + bias[None], NEG_INF)

    sink = sinks.astype(jnp.float32).reshape(A_KV_HEADS, A_GROUP)[None, None, :, :, None, None]
    sink = jnp.broadcast_to(sink, s.shape[:-1] + (1,))
    p = jax.nn.softmax(jnp.concatenate([s, sink], axis=-1), axis=-1)[..., :-1]
    o = jnp.einsum('bckgqs,bcskd->bcqkgd', p.astype(v.dtype), vb)
    return o.reshape(bsz, t, A_WIDTH)

def differential_attention(q, k, v, lam, lambda_init, subln_g):
    bsz, t = q.shape[0], q.shape[1]
    scale = 1.0 / math.sqrt(HEAD_DIM)
    slopes = alibi_slopes(B_HEADS)
    outs = []
    for i in range(t // B_QBLOCK):
        q0, kl = i * B_QBLOCK, (i + 1) * B_QBLOCK
        qs = q[:, q0:q0 + B_QBLOCK]
        ks, vs = k[:, :kl], v[:, :kl]
        s = jnp.einsum('bqhnd,bshnd->bhnqs', qs, ks).astype(jnp.float32) * scale
        q_pos = q0 + jnp.arange(B_QBLOCK)
        k_pos = jnp.arange(kl)
        dist = jnp.abs(q_pos[:, None] - k_pos[None, :]).astype(jnp.float32)
        allowed = (k_pos[None, :] // CHUNK) <= (q_pos[:, None] // CHUNK)
        s = jnp.where(allowed[None, None, None], s - slopes[None, :, None, None, None] * dist[None, None, None], NEG_INF)
        p = jax.nn.softmax(s, axis=-1)
        attn = p[:, :, 0] - lam * p[:, :, 1]
        outs.append(jnp.einsum('bhqs,bshe->bqhe', attn.astype(v.dtype), vs))
    o = jnp.concatenate(outs, axis=1)
    o = rmsnorm(o, subln_g) * (1.0 - lambda_init)
    return o.reshape(bsz, t, B_WIDTH).astype(v.dtype)

def hybrid_layer(x, layer, w_in, w_out, pre_g, post_g, sinks, lq1, lk1, lq2, lk2, subln_g):
    bsz, t, _ = x.shape
    h = rmsnorm(x, pre_g)
    p = jnp.einsum('btd,de->bte', h, w_in)
    aq, ak, av, ag, bq, bk, bv, bg = split_projection(p)

    ya = sliding_window_sink_attention(
        aq.reshape(bsz, t, A_HEADS, HEAD_DIM),
        ak.reshape(bsz, t, A_KV_HEADS, HEAD_DIM),
        av.reshape(bsz, t, A_KV_HEADS, HEAD_DIM), sinks)
    ya = ya * jax.nn.silu(ag)

    lambda_init = 0.8 - 0.6 * math.exp(-0.3 * layer)
    lam = (jnp.exp(jnp.sum(lq1.astype(jnp.float32) * lk1.astype(jnp.float32)))
           - jnp.exp(jnp.sum(lq2.astype(jnp.float32) * lk2.astype(jnp.float32))) + lambda_init)
    yb = differential_attention(
        bq.reshape(bsz, t, B_HEADS, 2, HEAD_DIM),
        bk.reshape(bsz, t, B_HEADS, 2, HEAD_DIM),
        bv.reshape(bsz, t, B_HEADS, B_VDIM), lam, lambda_init, subln_g)
    yb = yb * jax.nn.silu(bg)

    y = jnp.einsum('bte,ed->btd', jnp.concatenate([ya, yb], axis=-1), w_out)
    return x + rmsnorm(y, post_g)

def setup_inputs(seed: int = 0) -> dict:
    key = jax.random.key(seed)
    ks = jax.random.split(key, 12)
    f32 = jnp.float32
    return {
        "x": jax.random.normal(ks[0], (BATCH, SEQ, D_MODEL), f32),
        "w_in": jax.random.normal(ks[1], (DEPTH, D_MODEL, IN_WIDTH), f32) * D_MODEL ** -0.5,
        "w_out": jax.random.normal(ks[2], (DEPTH, MIX_WIDTH, D_MODEL), f32) * MIX_WIDTH ** -0.5,
        "pre_norm_g": 1.0 + 0.05 * jax.random.normal(ks[3], (DEPTH, D_MODEL), f32),
        "post_norm_g": 1.0 + 0.05 * jax.random.normal(ks[4], (DEPTH, D_MODEL), f32),
        "sinks": 0.5 * jax.random.normal(ks[5], (DEPTH, A_HEADS), f32),
        "lambda_q1": 0.1 * jax.random.normal(ks[6], (DEPTH, HEAD_DIM), f32),
        "lambda_k1": 0.1 * jax.random.normal(ks[7], (DEPTH, HEAD_DIM), f32),
        "lambda_q2": 0.1 * jax.random.normal(ks[8], (DEPTH, HEAD_DIM), f32),
        "lambda_k2": 0.1 * jax.random.normal(ks[9], (DEPTH, HEAD_DIM), f32),
        "subln_g": 1.0 + 0.05 * jax.random.normal(ks[10], (DEPTH, B_VDIM), f32),
    }

def reference(x, w_in, w_out, pre_norm_g, post_norm_g, sinks, lambda_q1, lambda_k1, lambda_q2, lambda_k2, subln_g):
    for layer in range(DEPTH):
        x = hybrid_layer(x, layer, w_in[layer], w_out[layer], pre_norm_g[layer], post_norm_g[layer],
                         sinks[layer], lambda_q1[layer], lambda_k1[layer], lambda_q2[layer],
                         lambda_k2[layer], subln_g[layer])
    return x


_drawn_inputs = setup_inputs


def setup_inputs(seed=0):
    import zlib

    import numpy as np

    out = dict(_drawn_inputs(seed))
    spreads = {}
    factors = {'sinks': 8.0, 'lambda_q1': 3.073, 'lambda_k2': 8.0}
    for name, (base, spread) in spreads.items():
        noise = np.random.default_rng([zlib.crc32(name.encode()), seed]).standard_normal(out[name].shape)
        drawn = base * np.exp(spread * noise) if base else spread * noise
        out[name] = __import__('jax').numpy.asarray(drawn.astype(out[name].dtype))
    for name, factor in factors.items():
        out[name] = (out[name] * factor).astype(out[name].dtype)
    return out
```

```python
import math

import concourse.bass as bass
from concourse import mybir

P = 128
SEQ, D_MODEL = 1024, 1024
CHUNK, HEAD_DIM = 64, 64
EPS = 1e-6
MASKED = -1e30
A_HEADS, A_KV = 8, 2
A_PAIRS = A_HEADS // A_KV
A_WIDTH = A_HEADS * HEAD_DIM
B_HEADS, B_WIDTH = 4, 512
TILES = SEQ // P
KT = D_MODEL // P
CHUNKS = SEQ // CHUNK
HALF = 512
LAMBDA_INIT = 0.8 - 0.6 * math.exp(-0.3 * 0)
SCALE = 1.0 / math.sqrt(HEAD_DIM)

AQ, AK = 0, A_WIDTH
AV = AK + A_KV * HEAD_DIM
AG = AV + A_KV * HEAD_DIM
BQ = AG + A_WIDTH
BK = BQ + B_WIDTH
BV = BK + B_WIDTH
BG = BV + B_WIDTH
IN_WIDTH = BG + B_WIDTH
V_WIDTH = B_WIDTH + A_KV * HEAD_DIM
VG = V_WIDTH // 2

UNITS = [("kB", 0), ("qB", 0), ("kB", 1), ("qB", 1), ("kA", 0), ("kB", 2), ("qB", 2), ("qA", 0),
         ("qA", 1), ("qA", 2), ("qA", 3), ("kB", 3), ("qB", 3), ("gB", 0), ("gB", 1), ("gB", 2),
         ("gA", 0), ("gA", 1), ("gA", 2), ("gA", 3), ("gB", 3)]
NU = len(UNITS)
GATES = [n for n, (kind, _) in enumerate(UNITS) if kind in ("gA", "gB")]
PLAIN = [n for n in range(NU) if n not in GATES]
PIECES = 3
RAW, SPLIT = 2, 3
LOADS = NU + KT
FIRST_PIECES = 12

B_UNITS = B_HEADS * TILES
B_PIECES = [1, 1, 1, 2, 2, 3, 3, 4]
A_PIECES = [1, 1]


def slope_a(h):
    return 2.0 ** (-8.0 * (h + 1) / A_HEADS)


def slope_b(h):
    return 2.0 ** (-8.0 * (h + 1) / B_HEADS)


def make_schedule():
    steps = []
    pieces = [(n, half, p) for n in range(NU) for half in range(2) for p in range(PIECES)]
    at = 0

    def take(count):
        nonlocal at
        for n, half, p in pieces[at:at + count]:
            if half == 0 and p == 0 and n + 2 < NU:
                steps.append(("split", n + 2))
            steps.append(("project", n, half, p))
        at = min(at + count, len(pieces))

    def rounds(u):
        return (u % TILES) // 4 + 1

    def b_slot(u, before, count):
        if before is not None:
            steps.append(("b_mix", before))
        if u is not None:
            done = at // (2 * PIECES)
            assert {("kB", u // TILES), ("qB", u // TILES)} <= set(UNITS[:done])
            steps.append(("b_scores", u))
        take((count + 1) // 2)
        count -= (count + 1) // 2
        if before is None:
            take(count)
            return
        for r in range(rounds(before)):
            steps.append(("b_transpose", before, r))
            if count:
                take(1)
                count -= 1
        steps.append(("b_values", before))
        if before % 4 == 1 and before > 4 and ("b_finish_transpose", before // 4 - 1) not in steps:
            steps.append(("b_finish_transpose", before // 4 - 1))
        if before % 4 == 3:
            steps.append(("b_finish", before // 4))
        take(count)

    def b_flush(u):
        b_slot(None, u, 3)
        take(1)
        steps.append(("b_finish_transpose", u // 4))

    def a_slot(c, before, count):
        if before is not None:
            steps.append(("a_weights", before))
        if c is not None:
            steps.append(("a_scores", c))
        take(count - count // 2)
        if before is not None:
            steps.append(("a_transpose", before))
            take(count // 2)
            steps.append(("a_values", before))

    steps += [("split", 0), ("split", 1)]
    take(FIRST_PIECES)
    before = None
    for u in range(3 * TILES):
        b_slot(u, before, B_PIECES[u % TILES])
        before = u
    b_flush(before)
    for c in range(CHUNKS):
        a_slot(c, c - 1 if c else None, A_PIECES[c % 2])
    a_slot(None, CHUNKS - 1, 2)
    before = None
    for u in range(3 * TILES, B_UNITS):
        b_slot(u, before, B_PIECES[u % TILES])
        before = u
    b_flush(before)
    last = (NU - 1) * 2 * PIECES
    outs = list(range(KT))
    while at < len(pieces):
        take(1)
        if outs and at % 2 == 0:
            steps.append(("split_out", outs.pop(0)))
        if at == last + PIECES + 1:
            steps += [("y_split", 0), ("y_split", 1)]
    steps += [("split_out", k) for k in outs]
    for t in range(TILES):
        if t + 2 < TILES:
            steps.append(("y_split", t + 2))
        steps += [("out_project", t, 0), ("out_project", t, 1), ("post", t)]
    return steps


SCHEDULE = make_schedule()


def order_of(kind, *which):
    same = [s[1:] for s in SCHEDULE if s[0] == kind]
    return same.index(which) + 1


def hybrid_layer(nc, x, w_in, w_out, pre_norm_g, post_norm_g, sinks, lambda_q1, lambda_k1,
                 lambda_q2, lambda_k2, subln_g, out):
    F32, F32R = mybir.dt.float32, mybir.dt.float32r
    ALU, ACT = mybir.AluOpType, mybir.ActivationFunctionType

    base = (nc.sbuf_base + 31) // 32 * 32
    KB = 1024

    def place(name, at_kb, shape, dtype=F32):
        return nc.alloc_sbuf_tensor_at(name, shape, dtype, offset=base + int(at_kb * KB))

    hT_hi = place("hT_hi", 0, [P, KT, SEQ], F32R)
    hT_lo = place("hT_lo", 32, [P, KT, SEQ], F32R)
    w_raw = place("w_raw", 64, [P, RAW, KT, P])
    w_hi = place("w_hi", 72, [P, SPLIT, KT, P], F32R)
    w_lo = place("w_lo", 84, [P, SPLIT, KT, P], F32R)
    v_sb = place("v_sb", 96, [P, TILES, V_WIDTH])
    v_shift = place("v_shift", 116, [P, TILES, P])
    kT_B = place("kT_B", 120, [P, 2, SEQ])
    kT_A = place("kT_A", 128, [P, CHUNK + SEQ])
    weights = place("weights", 132.25, [P, 2, 2, SEQ])
    weightsT = place("weightsT", 148.25, [P, 2, TILES, P])
    a_weights = place("a_weights", 156.25, [P, 2, A_PAIRS, P])
    a_weightsT = place("a_weightsT", 160.25, [P, A_PAIRS, P])
    qT_B = place("qT_B", 162.25, [P, B_HEADS, SEQ])
    qT_A = place("qT_A", 178.25, [P, A_PAIRS, SEQ])
    dist_b = place("dist_b", 194.25, [P, SEQ])
    dist_a = place("dist_a", 198.25, [P, 2, P])
    ident = place("ident", 199.25, [P, P])
    on_b = place("on_b", 199.75, [P, 4, P])
    gate = place("gate", 201.75, [P, 2, HALF])
    junk = place("junk", 205.75, [P, P])
    small = place("small", 206.25, [P, 352])
    wv_raw = place("wv_raw", 120, [P, KT, V_WIDTH])
    x_in = place("x_in", 140, [P, 2, D_MODEL])
    pre_g = place("pre_g", 148, [P, D_MODEL])
    wv_hi = place("wv_hi", 152, [P, KT, V_WIDTH], F32R)
    wv_lo = place("wv_lo", 172, [P, KT, V_WIDTH], F32R)
    wo_hi = place("wo_hi", 96, [P, KT, D_MODEL], F32R)
    wo_lo = place("wo_lo", 128, [P, KT, D_MODEL], F32R)
    post_g = place("post_g", 72, [P, D_MODEL])
    x_res = place("x_res", 76, [P, 2, D_MODEL])
    y_out = place("y_out", 84, [P, 2, D_MODEL])

    taken = [0]

    def column(width):
        taken[0] += width
        assert taken[0] <= 352
        return small[:, taken[0] - width:taken[0]]

    x_square = column(TILES)
    x_mean = column(TILES)
    x_scale = column(TILES)
    min_b = column(2 * B_UNITS)
    sum_b = column(2 * B_UNITS)
    inv_b = column(2 * B_UNITS)
    mix_b = column(B_UNITS)
    square_b = column(4)
    mean_b = column(4)
    rms_b = column(4)
    scale_b = column(4)
    min_a = column(2 * A_PAIRS)
    sum_a = column(2 * A_PAIRS)
    sink_arg = column(2 * A_PAIRS)
    sink_w = column(2 * A_PAIRS)
    total_a = column(2 * A_PAIRS)
    inv_a = column(2 * A_PAIRS)
    neg_half = column(4)
    sink = column(A_PAIRS)
    neg_sink = column(A_PAIRS)
    neg_slope = column(A_PAIRS)
    q_scale = column(A_PAIRS)
    sub_g = column(1)
    out_g = column(1)
    lam_dot = column(2)
    lam_exp = column(2)
    lam_dif = column(1)
    neg_lam = column(1)
    lam_in = gate
    y_square = square_b
    y_mean = mean_b
    y_scale = rms_b

    scores = nc.alloc_psum_tensor("scores", [P, 2048], F32)
    proj = nc.alloc_psum_tensor("proj", [P, 2, HALF], F32)
    banks = nc.alloc_psum_tensor("banks", [P, 1024], F32)
    turned = banks[:, 0:512]
    mixed = banks[:, 512:1024]

    def sem(name):
        return nc.alloc_semaphore(name)

    x_loaded = [sem("x_loaded0"), sem("x_loaded1")]
    wv_loaded = [sem(f"wv_loaded{i}") for i in range(4)]
    w_loaded = [sem(f"w_loaded{i}") for i in range(RAW)]
    pre_g_loaded = sem("pre_g_loaded")
    post_g_loaded = sem("post_g_loaded")
    small_loaded = sem("small_loaded")
    v_shifted = sem("v_shifted")
    res_loaded = [sem("res_loaded0"), sem("res_loaded1")]
    stored = [sem("stored0"), sem("stored1")]
    ident_made = sem("ident_made")
    dist_made = sem("dist_made")
    pads_made = sem("pads_made")
    half_made = sem("half_made")
    consts_made = sem("consts_made")
    slopes_made = sem("slopes_made")
    dist_ready = sem("dist_ready")
    lam_exped = sem("lam_exped")
    x_squared = sem("x_squared")
    x_meaned = sem("x_meaned")
    x_scaled = sem("x_scaled")
    x_normed = sem("x_normed")
    x_turned = sem("x_turned")
    h_hi_ready = sem("h_hi_ready")
    h_lo_ready = sem("h_lo_ready")
    wv_hi_ready = sem("wv_hi_ready")
    wv_lo_ready = sem("wv_lo_ready")
    v_projected = sem("v_projected")
    v_stored = sem("v_stored")
    w_hi_ready = sem("w_hi_ready")
    w_lo_ready = sem("w_lo_ready")
    projected = sem("projected")
    plain_stored = sem("plain_stored")
    tanh_done = sem("tanh_done")
    gate_done = sem("gate_done")
    gated = sem("gated")
    b_scored = sem("b_scored")
    b_biased = sem("b_biased")
    b_exped = sem("b_exped")
    b_inverted = sem("b_inverted")
    b_ratio = sem("b_ratio")
    b_mixed = sem("b_mixed")
    b_valued = sem("b_valued")
    b_squared = sem("b_squared")
    b_meaned = sem("b_meaned")
    b_rooted = sem("b_rooted")
    b_scaled = sem("b_scaled")
    turned_full = sem("turned_full")
    turned_read = sem("turned_read")
    mixed_read = sem("mixed_read")
    a_scored = sem("a_scored")
    a_biased = sem("a_biased")
    a_sinked = sem("a_sinked")
    a_exped = sem("a_exped")
    a_summed = sem("a_summed")
    a_inverted = sem("a_inverted")
    a_weighted = sem("a_weighted")
    a_valued = sem("a_valued")
    wo_hi_ready = sem("wo_hi_ready")
    wo_lo_ready = sem("wo_lo_ready")
    y_hi_ready = sem("y_hi_ready")
    y_lo_ready = sem("y_lo_ready")
    out_projected = sem("out_projected")
    y_squared = sem("y_squared")
    y_meaned = sem("y_meaned")
    y_rooted = sem("y_rooted")
    y_normed = sem("y_normed")
    y_added = sem("y_added")

    def halves_done(kind, index, half):
        return 2 * UNITS.index((kind, index)) + half + 1

    def plain_count(kind, index, half):
        return 2 * PLAIN.index(UNITS.index((kind, index))) + half + 1

    turned_users = [s for s in SCHEDULE
                    if s[0] in ("b_transpose", "b_finish_transpose", "a_transpose")]

    def turned_count(*step):
        return turned_users.index(step) + 1

    mixed_users = [s for s in SCHEDULE if s[0] == "a_values" or s[0] == "b_values" and s[1] % 4 == 3]

    def mixed_before(step):
        at = SCHEDULE.index(step)
        return sum(SCHEDULE.index(s) < at for s in mixed_users)

    def gate_count(n, half):
        return 2 * GATES.index(n) + half + 1

    def proj_user(n, half):
        return 2 * TILES + 2 * n + half

    def wait_proj_free(engine, filling):
        before = filling - 2
        if before < 0:
            return
        if before < 2 * TILES:
            engine.wait_ge(v_stored, before + 1)
            return
        n, half = divmod(before - 2 * TILES, 2)
        if n in GATES:
            engine.wait_ge(gate_done, gate_count(n, half))
        else:
            engine.wait_ge(plain_stored, plain_count(*UNITS[n], half))

    w_cols = w_in[0].rearrange("(k p) e -> p k e", p=P)

    def unit_columns(n):
        kind, i = UNITS[n]
        if kind == "kA":
            return [(AK, P)]
        if kind in ("qA", "gA"):
            first = (AQ if kind == "qA" else AG) + HEAD_DIM * i
            return [(first, HEAD_DIM), (first + A_PAIRS * HEAD_DIM, HEAD_DIM)]
        return [({"qB": BQ, "kB": BK, "gB": BG}[kind] + P * i, P)]

    def out_rows(k):
        if k < A_PAIRS:
            return [(HEAD_DIM * k, HEAD_DIM), (HEAD_DIM * (k + A_PAIRS), HEAD_DIM)]
        return [(P * k, P)]

    def load_count(n):
        total = 0
        for m in range(n % RAW, n + 1, RAW):
            total += 16 * len(unit_columns(m) if m < NU else out_rows(m - NU))
        return total

    def wo_raw(k):
        return w_raw[:, (NU + k) % RAW].rearrange("p k c -> p (k c)")

    v_runs = [[(BV, VG, 0)], [(BV + VG, B_WIDTH - VG, VG), (AV, P, B_WIDTH)]]

    with nc.Block() as block:

        @block.sync
        def _(sp):
            def load_x(t):
                if t >= 2:
                    sp.wait_ge(x_turned, t - 1)
                sp.dma_start(x_in[:, t % 2, :], x[0, t * P:(t + 1) * P, :]).then_inc(x_loaded[t % 2], 16)

            load_x(0)
            for part in range(2):
                k = slice(4 * part, 4 * part + 4)
                sp.dma_start(wv_raw[:, k, 0:VG], w_cols[:, k, BV:BV + VG]).then_inc(wv_loaded[part], 16)
                load_x(part + 1) if part == 0 else None
            for i, (first, count, to) in enumerate(v_runs[1]):
                sp.dma_start(wv_raw[:, :, to:to + count],
                             w_cols[:, :, first:first + count]).then_inc(wv_loaded[2 + i], 16)
                load_x(2 + i)

            def load_w(n):
                if n >= RAW:
                    before = n - RAW
                    if before < NU:
                        sp.wait_ge(w_hi_ready, before + 1)
                        sp.wait_ge(w_lo_ready, before + 1)
                    else:
                        sp.wait_ge(wo_hi_ready, before - NU + 1)
                        sp.wait_ge(wo_lo_ready, before - NU + 1)
                if n < NU:
                    to = 0
                    for first, count in unit_columns(n):
                        sp.dma_start(w_raw[:, n % RAW, :, to:to + count],
                                     w_cols[:, :, first:first + count]).then_inc(w_loaded[n % RAW], 16)
                        to += count
                else:
                    to = 0
                    for first, count in out_rows(n - NU):
                        sp.dma_start(wo_raw(n - NU)[to:to + count, :],
                                     w_out[0, first:first + count, :]).then_inc(w_loaded[n % RAW], 16)
                        to += count

            load_w(0)
            load_w(1)
            for t in range(4, TILES):
                load_x(t)
            sp.wait_ge(pads_made, 1)
            sp.wait_ge(v_stored, 2 * TILES)
            a_cols = slice(B_WIDTH, V_WIDTH)
            sp.dma_start(v_shift[CHUNK:P, :, :], v_sb[0:CHUNK, :, a_cols]).then_inc(v_shifted, 16)
            sp.dma_start(v_shift[0:CHUNK, 1:TILES, :],
                         v_sb[CHUNK:P, 0:TILES - 1, a_cols]).then_inc(v_shifted, 16)
            for n in range(2, LOADS):
                load_w(n)
            sp.wait_ge(projected, 2 * NU)
            sp.dma_start(post_g[:, :], post_norm_g[0:1, :].to_broadcast([P, D_MODEL])).then_inc(post_g_loaded, 16)
            for t in range(TILES):
                if t >= 2:
                    sp.wait_ge(y_added, 2 * t - 2)
                sp.dma_start(x_res[:, t % 2, :], x[0, t * P:(t + 1) * P, :]).then_inc(res_loaded[t % 2], 16)
            for t in range(2):
                sp.wait_ge(stored[t], 16 * 2 * (TILES // 2))

        @block.gpsimd
        def _(pool):
            def low_weights(n):
                pool.wait_ge(w_hi_ready, n + 1)
                nc.gpsimd.tensor_tensor(w_lo[:, n % SPLIT], w_raw[:, n % RAW],
                                        w_hi[:, n % SPLIT].bitcast(F32), ALU.subtract).then_inc(w_lo_ready, 1)

            nc.gpsimd.memset(ident[:, :], 0.0).then_inc(ident_made, 1)
            nc.gpsimd.memset(neg_half, -0.5).then_inc(half_made, 1)
            pool.wait_ge(ident_made, 1)
            nc.gpsimd.affine_select(out=ident[:, :], in_=ident[:, :], compare_op=ALU.not_equal, fill=1.0,
                                    base=0, pattern=[[-1, P]], channel_multiplier=1).then_inc(ident_made, 1)
            nc.gpsimd.iota(dist_b[:, :], [[-1, SEQ]], base=SEQ - P, channel_multiplier=1,
                           allow_small_or_imprecise_dtypes=True).then_inc(dist_made, 1)
            nc.gpsimd.iota(dist_a[:, 1, :], [[-1, P]], base=CHUNK, channel_multiplier=1,
                           allow_small_or_imprecise_dtypes=True).then_inc(dist_made, 1)

            def root(out_, in_, width, done):
                nc.gpsimd.tensor_tensor(out_, in_, neg_half[:, 0:width], ALU.pow).then_inc(done, 1)

            pool.wait_ge(half_made, 1)
            for t in range(TILES):
                pool.wait_ge(x_meaned, t + 1)
                root(x_scale[:, t:t + 1], x_mean[:, t:t + 1], 1, x_scaled)
                if t == TILES - 1:
                    for n in (0, 1):
                        low_weights(n)
            for step, *i in SCHEDULE:
                if step == "split" and i[0] >= 2:
                    low_weights(i[0])
                elif step == "split_out":
                    k = i[0]
                    pool.wait_ge(wo_hi_ready, k + 1)
                    nc.gpsimd.tensor_tensor(wo_lo[:, k, :], wo_raw(k), wo_hi[:, k, :].bitcast(F32),
                                            ALU.subtract).then_inc(wo_lo_ready, 1)
                elif step == "b_finish":
                    pool.wait_ge(b_meaned, i[0] + 1)
                    root(rms_b, mean_b, 4, b_rooted)
                elif step == "a_weights":
                    c = i[0]
                    pool.wait_ge(a_inverted, c + 1)
                    w = a_weights[:, c % 2]
                    r = inv_a[:, 4 * (c % 2):4 * (c % 2) + 4].unsqueeze(2).to_broadcast([P, A_PAIRS, P])
                    nc.gpsimd.tensor_tensor(w, w, r, ALU.mult).then_inc(a_weighted, 1)
                elif step == "post":
                    t = i[0]
                    pool.wait_ge(y_meaned, t + 1)
                    root(y_scale[:, t % 2:t % 2 + 1], y_mean[:, t % 2:t % 2 + 1], 1, y_rooted)

        @block.scalar
        def _(act):
            act.dma_start(pre_g[:, :], pre_norm_g[0:1, :].to_broadcast([P, D_MODEL])).then_inc(pre_g_loaded, 16)
            for h, part in enumerate((slice(0, CHUNK), slice(CHUNK, P))):
                act.dma_start(sink[part, :], sinks[0:1, 4 * h:4 * h + 4].to_broadcast([CHUNK, 4])).then_inc(small_loaded, 16)
            act.dma_start(sub_g, subln_g.rearrange("a e -> e a")).then_inc(small_loaded, 16)
            for v, vector in enumerate((lambda_q1, lambda_k1, lambda_q2, lambda_k2)):
                act.dma_start(lam_in[:, 0, HEAD_DIM * v:HEAD_DIM * (v + 1)],
                              vector[0:1, :].to_broadcast([P, HEAD_DIM])).then_inc(small_loaded, 16)

            def high_wv(k, cols, ready):
                act.wait_ge(wv_loaded[ready], 16)
                nc.scalar.activation(wv_hi[:, k, cols], wv_raw[:, k, cols], ACT.Copy).then_inc(wv_hi_ready, 1)

            def high_h(t):
                act.wait_ge(x_turned, t + 1)
                nc.scalar.activation(hT_hi[:, :, t * P:(t + 1) * P],
                                     scores[:, 1024 * (t % 2):1024 * (t % 2) + 1024].rearrange("p (k c) -> p k c", c=P),
                                     ACT.Copy).then_inc(h_hi_ready, 1)

            def square_x(t):
                act.wait_ge(x_loaded[t % 2], 16 * (t // 2 + 1))
                if t:
                    act.wait_ge(x_squared, t)
                nc.scalar.activation(banks[:, :], x_in[:, t % 2, :], ACT.Square, scale=D_MODEL ** -0.5,
                                     accum_out=x_square[:, t:t + 1]).then_inc(x_squared, 1)

            def store_v(t, g):
                n = TILES * g + t
                act.wait_ge(v_projected, n + 1)
                nc.scalar.activation(v_sb[:, t, VG * g:VG * (g + 1)], proj[:, n % 2, 0:VG],
                                     ACT.Copy).then_inc(v_stored, 1)

            def high_weights(n):
                act.wait_ge(w_loaded[n % RAW], load_count(n))
                if n >= SPLIT:
                    act.wait_ge(projected, 2 * (n - SPLIT) + 2)
                nc.scalar.activation(w_hi[:, n % SPLIT], w_raw[:, n % RAW], ACT.Copy).then_inc(w_hi_ready, 1)

            square_x(0)
            high_wv(slice(0, 4), slice(0, VG), 0)
            square_x(1)
            high_h(0)
            high_wv(slice(4, 8), slice(0, VG), 1)
            for t in range(TILES):
                if t + 2 < TILES:
                    square_x(t + 2)
                if t + 1 < TILES:
                    high_h(t + 1)
                store_v(t, 0)
                if t == 2:
                    high_wv(slice(0, 8), slice(VG, B_WIDTH), 2)
                if t == 3:
                    high_wv(slice(0, 8), slice(B_WIDTH, V_WIDTH), 3)
                if t in (5, 6):
                    high_weights(t - 5)
                if t == 7:
                    act.wait_ge(consts_made, 2)
                    nc.scalar.activation(lam_exp, lam_dot, ACT.Exp).then_inc(lam_exped, 1)
            for t in range(TILES):
                store_v(t, 1)

            for step, *i in SCHEDULE:
                if step == "split" and i[0] >= 2:
                    high_weights(i[0])
                elif step == "split_out":
                    k = i[0]
                    act.wait_ge(w_loaded[(NU + k) % RAW], load_count(NU + k))
                    act.wait_ge(turned_full, len(turned_users))
                    nc.scalar.activation(wo_hi[:, k, :], wo_raw(k), ACT.Copy).then_inc(wo_hi_ready, 1)
                elif step == "project" and i[2] == PIECES - 1:
                    n, half, _ = i
                    kind, head = UNITS[n]
                    source = proj[:, proj_user(n, half) % 2, :]
                    tokens = slice(HALF * half, HALF * half + HALF)
                    act.wait_ge(projected, 2 * n + half + 1)
                    if kind == "kB":
                        to = kT_B[:, head % 2, tokens]
                        nc.scalar.activation(to, source, ACT.Copy).then_inc(plain_stored, 1)
                    elif kind == "kA":
                        to = kT_A[:, CHUNK + HALF * half:CHUNK + HALF * half + HALF]
                        nc.scalar.activation(to, source, ACT.Copy).then_inc(plain_stored, 1)
                    elif kind == "qB":
                        nc.scalar.activation(qT_B[:, head, tokens], source, ACT.Copy,
                                             scale=SCALE / slope_b(head)).then_inc(plain_stored, 1)
                    elif kind == "qA":
                        act.wait_ge(slopes_made, 4 * A_PAIRS)
                        nc.scalar.activation(qT_A[:, head, tokens], source, ACT.Copy,
                                             scale=q_scale[:, head:head + 1]).then_inc(plain_stored, 1)
                    else:
                        g = gate_count(n, half) - 1
                        if g >= 2:
                            act.wait_ge(gated, g - 1)
                        nc.scalar.activation(gate[:, g % 2, :], source, ACT.Tanh, scale=0.5).then_inc(tanh_done, 1)
                elif step == "b_scores":
                    u = i[0]
                    keys = P * (u % TILES + 1)
                    for m in range(2):
                        w = weights[:, u % 2, m, 0:keys]
                        act.wait_ge(b_biased, 2 * u + m + 1)
                        nc.scalar.activation(w, w, ACT.Exp, scale=-1.0, bias=min_b[:, 2 * u + m:2 * u + m + 1],
                                             accum_out=sum_b[:, 2 * u + m:2 * u + m + 1]).then_inc(b_exped, 1)
                elif step == "b_transpose":
                    u, r = i
                    blocks = min(4, u % TILES + 1 - 4 * r)
                    if u >= 2:
                        act.wait_ge(b_valued, u - 1)
                    act.wait_ge(turned_full, turned_count("b_transpose", u, r))
                    nc.scalar.activation(weightsT[:, u % 2, 4 * r:4 * r + blocks, :],
                                         turned[:, 0:P * blocks].rearrange("p (b q) -> p b q", q=P),
                                         ACT.Copy).then_inc(turned_read, 1)
                elif step == "b_finish":
                    f = i[0]
                    act.wait_ge(b_valued, 4 * f + 4)
                    if f:
                        act.wait_ge(b_meaned, f)
                    for j in range(4):
                        u = 4 * f + j
                        if 4 * f + j:
                            act.wait_ge(b_squared, 4 * f + j)
                        nc.scalar.activation(junk[:, :], mixed[:, P * j:P * j + P], ACT.Square,
                                             scale=inv_b[:, 2 * u:2 * u + 1],
                                             accum_out=square_b[:, j:j + 1]).then_inc(b_squared, 1)
                elif step == "b_finish_transpose":
                    f = i[0]
                    act.wait_ge(turned_full, turned_count("b_finish_transpose", f))
                    act.wait_ge(consts_made, 4)
                    nc.scalar.activation(qT_B[:, f // 2, HALF * (f % 2):HALF * (f % 2) + HALF], turned[:, :],
                                         ACT.Copy, scale=out_g).then_inc(turned_read, 1)
                elif step == "a_scores":
                    c = i[0]
                    s = 4 * (c % 2)
                    for j in range(A_PAIRS):
                        w = a_weights[:, c % 2, j, :]
                        act.wait_ge(a_biased, 4 * c + j + 1)
                        nc.scalar.activation(w, w, ACT.Exp, scale=-1.0, bias=min_a[:, s + j:s + j + 1],
                                             accum_out=sum_a[:, s + j:s + j + 1]).then_inc(a_exped, 1)
                    act.wait_ge(a_sinked, c + 1)
                    nc.scalar.activation(sink_w[:, s:s + 4], sink_arg[:, s:s + 4], ACT.Exp).then_inc(a_exped, 1)
                elif step == "a_transpose":
                    c = i[0]
                    if c:
                        act.wait_ge(a_valued, c)
                    act.wait_ge(turned_full, turned_count("a_transpose", c))
                    nc.scalar.activation(a_weightsT[:, :, :], turned[:, :].rearrange("p (j q) -> p j q", q=P),
                                         ACT.Copy).then_inc(turned_read, 1)
                elif step == "y_split":
                    t = i[0]
                    tokens = slice(P * t, P * t + P)
                    half = t // 4
                    act.wait_ge(projected, 2 * NU - 1 + half)
                    act.wait_ge(gated, 2 * len(GATES) - 1 + half)
                    for first, part in ((0, qT_A), (A_PAIRS, qT_B)):
                        nc.scalar.activation(hT_hi[:, first:first + 4, tokens], part[:, :, tokens],
                                             ACT.Copy).then_inc(y_hi_ready, 1)
                elif step == "out_project":
                    t, half = i
                    act.wait_ge(out_projected, 2 * t + half + 1)
                    if t >= 2:
                        act.wait_ge(y_meaned, t - 1)
                    if 2 * t + half:
                        act.wait_ge(y_squared, 2 * t + half)
                    at = 1024 * (t % 2) + HALF * half
                    nc.scalar.activation(turned, scores[:, at:at + HALF], ACT.Square, scale=D_MODEL ** -0.5,
                                         accum_out=y_square[:, 2 * (t % 2) + half:2 * (t % 2) + half + 1]).then_inc(y_squared, 1)
                elif step == "post":
                    t = i[0]
                    for half in range(2):
                        act.wait_ge(y_added, 2 * t + half + 1)
                        cols = slice(HALF * half, HALF * half + HALF)
                        act.dma_start(out[0, P * t:P * t + P, cols], y_out[:, t % 2, cols]).then_inc(stored[t % 2], 16)

        @block.vector
        def _(dve):
            def mean_x(t):
                dve.wait_ge(x_squared, t + 1)
                nc.vector.tensor_scalar(x_mean[:, t:t + 1], x_square[:, t:t + 1], EPS, None, ALU.add).then_inc(x_meaned, 1)

            def norm_x(t):
                if t == 0:
                    dve.wait_ge(pre_g_loaded, 16)
                dve.wait_ge(x_scaled, t + 1)
                nc.vector.scalar_tensor_tensor(x_in[:, t % 2, :], x_in[:, t % 2, :], x_scale[:, t:t + 1],
                                               pre_g[:, :], ALU.mult, ALU.mult).then_inc(x_normed, 1)

            def low_h(t):
                dve.wait_ge(h_hi_ready, t + 1)
                tokens = slice(P * t, P * t + P)
                s = scores[:, 1024 * (t % 2):1024 * (t % 2) + 1024].rearrange("p (k c) -> p k c", c=P)
                nc.vector.tensor_tensor(hT_lo[:, :, tokens], s, hT_hi[:, :, tokens].bitcast(F32),
                                        ALU.subtract).then_inc(h_lo_ready, 1)

            def low_wv(k, cols, part):
                dve.wait_ge(wv_hi_ready, part + 1)
                nc.vector.tensor_tensor(wv_lo[:, k, cols], wv_raw[:, k, cols], wv_hi[:, k, cols].bitcast(F32),
                                        ALU.subtract).then_inc(wv_lo_ready, 1)

            def constants():
                dve.wait_ge(small_loaded, 16 * 7)
                for d in range(2):
                    a, b = (lam_in[:, 0, HEAD_DIM * v:HEAD_DIM * (v + 1)] for v in (2 * d, 2 * d + 1))
                    nc.vector.tensor_tensor_reduce(out=on_b[:, d, 0:HEAD_DIM], in0=a, in1=b, scale=1.0, scalar=0.0,
                                                   op0=ALU.mult, op1=ALU.add,
                                                   accum_out=lam_dot[:, d:d + 1]).then_inc(consts_made, 1)
                nc.vector.tensor_scalar(neg_sink, sink, -1.0, None, ALU.mult).then_inc(consts_made, 1)
                nc.vector.tensor_scalar(out_g, sub_g, 0.5 * (1.0 - LAMBDA_INIT), None, ALU.mult).then_inc(consts_made, 1)
                for j in range(A_PAIRS):
                    for h, part in ((j, slice(0, CHUNK)), (j + A_PAIRS, slice(CHUNK, P))):
                        nc.vector.memset(q_scale[part, j:j + 1], SCALE / slope_a(h)).then_inc(slopes_made, 1)
                        nc.vector.memset(neg_slope[part, j:j + 1], -slope_a(h)).then_inc(slopes_made, 1)
                nc.vector.memset(v_shift[0:CHUNK, 0, :], 0.0).then_inc(pads_made, 1)
                dve.wait_ge(dist_made, 2)
                lower = dist_a[CHUNK:P, 1, :]
                nc.vector.tensor_scalar(lower, lower, float(CHUNK), None, ALU.subtract).then_inc(dist_ready, 1)
                dve.wait_ge(dist_ready, 1)
                for d in (dist_b[:, :], dist_a[:, 1, :]):
                    nc.vector.scalar_tensor_tensor(d, d, -1.0, d, ALU.mult, ALU.min).then_inc(dist_ready, 1)
                dve.wait_ge(dist_ready, 3)
                nc.vector.memset(dist_b[0:CHUNK, SEQ - CHUNK:SEQ], MASKED).then_inc(dist_ready, 1)
                nc.vector.tensor_copy(dist_a[:, 0, CHUNK:P], dist_a[:, 1, CHUNK:P]).then_inc(dist_ready, 1)
                nc.vector.memset(dist_a[:, 0, 0:CHUNK], MASKED).then_inc(dist_ready, 1)

            def make_lambda():
                dve.wait_ge(lam_exped, 1)
                nc.vector.tensor_tensor(lam_dif, lam_exp[:, 1:2], lam_exp[:, 0:1], ALU.subtract).then_inc(consts_made, 1)
                dve.wait_ge(consts_made, 5)
                nc.vector.tensor_scalar(neg_lam, lam_dif, LAMBDA_INIT, None, ALU.subtract).then_inc(consts_made, 1)

            mean_x(0)
            norm_x(0)
            low_wv(slice(0, 4), slice(0, VG), 0)
            mean_x(1)
            norm_x(1)
            low_h(0)
            low_wv(slice(4, 8), slice(0, VG), 1)
            for t in range(TILES):
                if t + 2 < TILES:
                    mean_x(t + 2)
                    norm_x(t + 2)
                if t + 1 < TILES:
                    low_h(t + 1)
                if t == 2:
                    low_wv(slice(0, 8), slice(VG, B_WIDTH), 2)
                if t == 3:
                    low_wv(slice(0, 8), slice(B_WIDTH, V_WIDTH), 3)
                if t == 5:
                    constants()
            make_lambda()
            dve.wait_ge(v_projected, 2 * TILES)
            nc.vector.memset(kT_A[:, 0:CHUNK], 0.0).then_inc(pads_made, 1)
            dve.wait_ge(dist_ready, 6)

            for step, *i in SCHEDULE:
                if step == "project" and i[2] == PIECES - 1 and i[0] in GATES:
                    n, half, _ = i
                    kind, head = UNITS[n]
                    g = gate_count(n, half) - 1
                    tokens = slice(HALF * half, HALF * half + HALF)
                    source = proj[:, proj_user(n, half) % 2, :]
                    o = (qT_A if kind == "gA" else qT_B)[:, head, tokens]
                    dve.wait_ge(tanh_done, g + 1)
                    nc.vector.scalar_tensor_tensor(gate[:, g % 2, :], gate[:, g % 2, :], 1.0, source,
                                                   ALU.add, ALU.mult).then_inc(gate_done, 1)
                    dve.wait_ge(gate_done, g + 1)
                    if kind == "gB":
                        dve.wait_ge(turned_read, turned_count("b_finish_transpose", 2 * head + half))
                    else:
                        dve.wait_ge(mixed_read, mixed_users.index(("a_values", CHUNKS - 1)) + 1)
                    nc.vector.tensor_tensor(o, gate[:, g % 2, :], o, ALU.mult).then_inc(gated, 1)
                elif step == "b_mix":
                    u = i[0]
                    keys = P * (u % TILES + 1)
                    dve.wait_ge(b_exped, 2 * u + 2)
                    pair = slice(2 * u, 2 * u + 2)
                    nc.vector.reciprocal(inv_b[:, pair], sum_b[:, pair]).then_inc(b_inverted, 1)
                    dve.wait_ge(b_inverted, u + 1)
                    nc.vector.tensor_scalar(mix_b[:, u:u + 1], sum_b[:, 2 * u:2 * u + 1], inv_b[:, 2 * u + 1:2 * u + 2],
                                            neg_lam, ALU.mult, ALU.mult).then_inc(b_ratio, 1)
                    dve.wait_ge(b_ratio, u + 1)
                    w0, w1 = (weights[:, u % 2, m, 0:keys] for m in range(2))
                    nc.vector.scalar_tensor_tensor(w0, w1, mix_b[:, u:u + 1], w0, ALU.mult, ALU.add).then_inc(b_mixed, 1)
                elif step == "b_scores":
                    u = i[0]
                    keys = P * (u % TILES + 1)
                    if u >= 2:
                        dve.wait_ge(turned_full, turned_count("b_transpose", u - 2, ((u - 2) % TILES) // 4))
                        dve.wait_ge(b_mixed, u - 1)
                    for m in range(2):
                        dve.wait_ge(b_scored, 2 * u + m + 1)
                        nc.vector.tensor_tensor_reduce(
                            out=weights[:, u % 2, m, 0:keys], in0=scores[:, 1024 * m:1024 * m + keys],
                            in1=dist_b[:, SEQ - keys:SEQ], scale=-slope_b(u // TILES), scalar=-MASKED,
                            op0=ALU.add, op1=ALU.min,
                            accum_out=min_b[:, 2 * u + m:2 * u + m + 1]).then_inc(b_biased, 1)
                elif step == "b_finish":
                    f = i[0]
                    dve.wait_ge(b_squared, 4 * f + 4)
                    nc.vector.tensor_scalar(mean_b, square_b, 1.0 / P, EPS, ALU.mult, ALU.add).then_inc(b_meaned, 1)
                    dve.wait_ge(b_rooted, f + 1)
                    nc.vector.tensor_tensor(scale_b, rms_b, inv_b[:, 8 * f:8 * f + 8].rearrange("p (u m) -> p u m", m=2)[:, :, 0],
                                            ALU.mult).then_inc(b_scaled, 1)
                    dve.wait_ge(b_scaled, f + 1)
                    if f:
                        dve.wait_ge(turned_full, turned_count("b_finish_transpose", f - 1))
                    nc.vector.tensor_tensor(on_b[:, :, :], mixed.rearrange("p (u e) -> p u e", e=P),
                                            scale_b.unsqueeze(2).to_broadcast([P, 4, P]), ALU.mult).then_inc(mixed_read, 1)
                elif step == "a_scores":
                    c = i[0]
                    s = 4 * (c % 2)
                    if c == 0:
                        dve.wait_ge(slopes_made, 4 * A_PAIRS)
                    if c >= 2:
                        dve.wait_ge(turned_full, turned_count("a_transpose", c - 2))
                    dve.wait_ge(a_scored, c + 1)
                    for j in range(A_PAIRS):
                        nc.vector.tensor_tensor_reduce(
                            out=a_weights[:, c % 2, j, :], in0=scores[:, 512 * (c % 4) + P * j:512 * (c % 4) + P * (j + 1)],
                            in1=dist_a[:, min(c, 1), :], scale=neg_slope[:, j:j + 1], scalar=neg_sink[:, j:j + 1],
                            op0=ALU.add, op1=ALU.min, accum_out=min_a[:, s + j:s + j + 1]).then_inc(a_biased, 1)
                    dve.wait_ge(a_biased, 4 * c + 4)
                    nc.vector.tensor_tensor(sink_arg[:, s:s + 4], min_a[:, s:s + 4], sink, ALU.add).then_inc(a_sinked, 1)
                elif step == "a_weights":
                    c = i[0]
                    s = 4 * (c % 2)
                    dve.wait_ge(a_exped, 5 * c + 5)
                    nc.vector.tensor_tensor(total_a[:, s:s + 4], sum_a[:, s:s + 4], sink_w[:, s:s + 4], ALU.add).then_inc(a_summed, 1)
                    dve.wait_ge(a_summed, c + 1)
                    nc.vector.reciprocal(inv_a[:, s:s + 4], total_a[:, s:s + 4]).then_inc(a_inverted, 1)
                elif step == "a_values":
                    c = i[0]
                    dve.wait_ge(a_valued, c + 1)
                    nc.vector.tensor_scalar(qT_A[:, :, CHUNK * c:CHUNK * c + CHUNK],
                                            mixed[:, 0:A_PAIRS * CHUNK].rearrange("p (j q) -> p j q", q=CHUNK),
                                            0.5, None, ALU.mult).then_inc(mixed_read, 1)
                elif step == "y_split":
                    t = i[0]
                    tokens = slice(P * t, P * t + P)
                    for p, (first, part) in enumerate(((0, qT_A), (A_PAIRS, qT_B))):
                        dve.wait_ge(y_hi_ready, 2 * t + p + 1)
                        nc.vector.tensor_tensor(hT_lo[:, first:first + 4, tokens], part[:, :, tokens],
                                                hT_hi[:, first:first + 4, tokens].bitcast(F32),
                                                ALU.subtract).then_inc(y_lo_ready, 1)
                elif step == "post":
                    t = i[0]
                    dve.wait_ge(y_squared, 2 * t + 2)
                    s = 2 * (t % 2)
                    nc.vector.scalar_tensor_tensor(y_mean[:, t % 2:t % 2 + 1], y_square[:, s:s + 1], EPS,
                                                   y_square[:, s + 1:s + 2], ALU.add, ALU.add).then_inc(y_meaned, 1)
                    if t == 0:
                        dve.wait_ge(post_g_loaded, 16)
                    if t >= 2:
                        dve.wait_ge(stored[t % 2], 32 * (t // 2))
                    dve.wait_ge(y_rooted, t + 1)
                    for half in range(2):
                        cols = slice(HALF * half, HALF * half + HALF)
                        at = 1024 * (t % 2) + HALF * half
                        nc.vector.scalar_tensor_tensor(y_out[:, t % 2, cols], scores[:, at:at + HALF],
                                                       y_scale[:, t % 2:t % 2 + 1], post_g[:, cols],
                                                       ALU.mult, ALU.mult).then_inc(y_normed, 1)
                    dve.wait_ge(res_loaded[t % 2], 16 * (t // 2 + 1))
                    for half in range(2):
                        cols = slice(HALF * half, HALF * half + HALF)
                        dve.wait_ge(y_normed, 2 * t + half + 1)
                        nc.vector.tensor_tensor(y_out[:, t % 2, cols], y_out[:, t % 2, cols],
                                                x_res[:, t % 2, cols], ALU.add).then_inc(y_added, 1)

        @block.tensor
        def _(pe):
            def turn_x(t):
                pe.wait_ge(x_normed, t + 1)
                if t >= 2:
                    pe.wait_ge(h_lo_ready, t - 1)
                for k in range(KT):
                    at = 1024 * (t % 2) + P * k
                    last = nc.tensor.transpose(scores[:, at:at + P], x_in[:, t % 2, P * k:P * k + P], ident[:, :])
                last.then_inc(x_turned, 1)

            def project_v(t, g):
                n = TILES * g + t
                wait_proj_free(pe, n)
                pe.wait_ge(h_lo_ready, t + 1)
                pe.wait_ge(wv_lo_ready, 2 * g + 2)
                tokens, cols = slice(P * t, P * t + P), slice(VG * g, VG * (g + 1))
                for p, (h, w) in enumerate(((hT_hi, wv_hi), (hT_lo, wv_hi), (hT_hi, wv_lo))):
                    for k in range(KT):
                        last = nc.tensor.matmul(proj[:, n % 2, 0:VG], h[:, k, tokens], w[:, k, cols],
                                                start=(p == 0 and k == 0), stop=(p == PIECES - 1 and k == KT - 1))
                last.then_inc(v_projected, 1)

            pe.wait_ge(ident_made, 2)
            turn_x(0)
            turn_x(1)
            for t in range(TILES):
                project_v(t, 0)
                if t + 2 < TILES:
                    turn_x(t + 2)
            for t in range(TILES):
                project_v(t, 1)

            for step, *i in SCHEDULE:
                if step == "project":
                    n, half, p = i
                    to = proj[:, proj_user(n, half) % 2, :]
                    slot = n % SPLIT
                    if p == 0:
                        wait_proj_free(pe, proj_user(n, half))
                        pe.wait_ge(w_hi_ready, n + 1)
                    if p == PIECES - 1:
                        pe.wait_ge(w_lo_ready, n + 1)
                    w, h = ((w_hi, hT_hi), (w_hi, hT_lo), (w_lo, hT_hi))[p]
                    for k in range(KT):
                        last = nc.tensor.matmul(to, w[:, slot, k, :], h[:, k, HALF * half:HALF * half + HALF],
                                                start=(p == 0 and k == 0), stop=(p == PIECES - 1 and k == KT - 1))
                    if p == PIECES - 1:
                        last.then_inc(projected, 1)
                elif step == "b_scores":
                    u = i[0]
                    head, block_ = divmod(u, TILES)
                    keys = P * (block_ + 1)
                    pe.wait_ge(plain_stored, plain_count("qB", head, block_ // 4))
                    if u == 3 * TILES:
                        pe.wait_ge(a_biased, A_PAIRS * CHUNKS)
                    for m in range(2):
                        if u:
                            pe.wait_ge(b_biased, 2 * u - 1 + m)
                        part = slice(HEAD_DIM * m, HEAD_DIM * (m + 1))
                        for first in range(0, keys, HALF):
                            width = min(HALF, keys - first)
                            last = nc.tensor.matmul(scores[:, 1024 * m + first:1024 * m + first + width],
                                                    qT_B[part, head, P * block_:P * block_ + P],
                                                    kT_B[part, head % 2, first:first + width], start=True, stop=True)
                        last.then_inc(b_scored, 1)
                elif step == "b_transpose":
                    u, r = i
                    pe.wait_ge(b_mixed, u + 1)
                    pe.wait_ge(turned_read, turned_count("b_transpose", u, r) - 1) if turned_count("b_transpose", u, r) > 1 else None
                    for b in range(4 * r, min(4 * r + 4, u % TILES + 1)):
                        last = nc.tensor.transpose(turned[:, P * (b - 4 * r):P * (b - 4 * r) + P],
                                                   weights[:, u % 2, 0, P * b:P * b + P], ident[:, :])
                    last.then_inc(turned_full, 1)
                elif step == "b_values":
                    u = i[0]
                    head, blocks = u // TILES, u % TILES + 1
                    pe.wait_ge(turned_read, turned_count("b_transpose", u, (blocks - 1) // 4))
                    if u % 4 == 0 and mixed_before((step, *i)):
                        pe.wait_ge(mixed_read, mixed_before((step, *i)))
                    for b in range(blocks):
                        last = nc.tensor.matmul(mixed[:, P * (u % 4):P * (u % 4) + P], weightsT[:, u % 2, b, :],
                                                v_sb[:, b, P * head:P * head + P], start=(b == 0), stop=(b == blocks - 1))
                    last.then_inc(b_valued, 1)
                elif step == "b_finish_transpose":
                    f = i[0]
                    pe.wait_ge(mixed_read, mixed_users.index(("b_values", 4 * f + 3)) + 1)
                    pe.wait_ge(turned_read, turned_count(step, f) - 1)
                    for j in range(4):
                        last = nc.tensor.transpose(turned[:, P * j:P * j + P], on_b[:, j, :], ident[:, :])
                    last.then_inc(turned_full, 1)
                elif step == "a_scores":
                    c = i[0]
                    if c == 0:
                        pe.wait_ge(pads_made, 2)
                        pe.wait_ge(v_shifted, 32)
                        pe.wait_ge(plain_stored, plain_count("qA", A_PAIRS - 1, 1))
                        pe.wait_ge(b_biased, 2 * 3 * TILES)
                    if c >= 4:
                        pe.wait_ge(a_biased, A_PAIRS * (c - 3))
                    for j in range(A_PAIRS):
                        for h in range(2):
                            part = slice(HEAD_DIM * h, HEAD_DIM * (h + 1))
                            at = 512 * (c % 4) + P * j
                            last = nc.tensor.matmul(scores[part, at:at + P], qT_A[part, j, CHUNK * c:CHUNK * c + CHUNK],
                                                    kT_A[part, CHUNK * c:CHUNK * c + P], start=True, stop=True)
                    last.then_inc(a_scored, 1)
                elif step == "a_transpose":
                    c = i[0]
                    pe.wait_ge(a_weighted, c + 1)
                    pe.wait_ge(turned_read, turned_count(step, c) - 1)
                    for j in range(A_PAIRS):
                        last = nc.tensor.transpose(turned[:, P * j:P * j + P], a_weights[:, c % 2, j, :], ident[:, :])
                    last.then_inc(turned_full, 1)
                elif step == "a_values":
                    c = i[0]
                    pe.wait_ge(turned_read, turned_count("a_transpose", c))
                    pe.wait_ge(mixed_read, mixed_before((step, *i)))
                    for h in range(2):
                        part = slice(HEAD_DIM * h, HEAD_DIM * (h + 1))
                        v = v_sb[:, c // 2, B_WIDTH:V_WIDTH] if c % 2 else v_shift[:, c // 2, :]
                        last = nc.tensor.matmul(mixed[part, 0:A_PAIRS * CHUNK], v[:, part],
                                                a_weightsT[:, :, part], start=True, stop=True)
                    last.then_inc(a_valued, 1)
                elif step == "out_project":
                    t, half = i
                    tokens, cols = slice(P * t, P * t + P), slice(HALF * half, HALF * half + HALF)
                    pe.wait_ge(y_lo_ready, 2 * t + 2)
                    if t >= 2:
                        pe.wait_ge(y_normed, 2 * (t - 2) + half + 1)
                    at = 1024 * (t % 2) + HALF * half
                    for p, (y, w) in enumerate(((hT_hi, wo_hi), (hT_lo, wo_hi), (hT_hi, wo_lo))):
                        for k in range(KT):
                            if t == 0 and half == 0 and p != 1:
                                pe.wait_ge(wo_lo_ready if p else wo_hi_ready, k + 1)
                            last = nc.tensor.matmul(scores[:, at:at + HALF], y[:, k, tokens], w[:, k, cols],
                                                    start=(p == 0 and k == 0), stop=(p == PIECES - 1 and k == KT - 1))
                    last.then_inc(out_projected, 1)


INPUTS = ["x", "w_in", "w_out", "pre_norm_g", "post_norm_g", "sinks", "lambda_q1", "lambda_k1",
          "lambda_q2", "lambda_k2", "subln_g"]


def kernel(**inputs):
    import concourse.bacc as bacc
    import numpy as np
    from concourse.bass_utils import run_bass_kernel_spmd

    nc = bacc.Bacc("TRN2", target_bir_lowering=False, num_devices=1)
    arrays = {f"in_{name}": np.ascontiguousarray(inputs[name]) for name in INPUTS}
    args = [nc.dram_tensor(name, a.shape, mybir.dt.from_np(a.dtype), kind="ExternalInput").ap()
            for name, a in arrays.items()]
    out = nc.dram_tensor("out", (1, SEQ, D_MODEL), mybir.dt.float32, kind="ExternalOutput").ap()
    hybrid_layer(nc, *args, out)
    result = run_bass_kernel_spmd(nc, [arrays], core_ids=[0])
    return result.results[0]["out"]
```

```python
import math

import concourse.bass as bass
from concourse import mybir

P = 128
SEQ, D_MODEL = 1024, 1024
CHUNK, HEAD_DIM = 64, 64
EPS = 1e-6
MASKED = -1e30
A_HEADS, A_KV = 8, 2
A_PAIRS = A_HEADS // A_KV
A_WIDTH = A_HEADS * HEAD_DIM
B_HEADS, B_WIDTH = 4, 512
TILES = SEQ // P
KT = D_MODEL // P
CHUNKS = SEQ // CHUNK
HALF = 512
LAMBDA_INIT = 0.8 - 0.6 * math.exp(-0.3 * 0)
SCALE = 1.0 / math.sqrt(HEAD_DIM)

AQ, AK = 0, A_WIDTH
AV = AK + A_KV * HEAD_DIM
AG = AV + A_KV * HEAD_DIM
BQ = AG + A_WIDTH
BK = BQ + B_WIDTH
BV = BK + B_WIDTH
BG = BV + B_WIDTH
IN_WIDTH = BG + B_WIDTH
V_WIDTH = B_WIDTH + A_KV * HEAD_DIM
VG = V_WIDTH // 2

UNITS = [("kB", 0), ("qB", 0), ("kB", 1), ("qB", 1), ("kA", 0), ("kB", 2), ("qB", 2), ("qA", 0),
         ("qA", 1), ("qA", 2), ("qA", 3), ("kB", 3), ("qB", 3), ("gB", 0), ("gB", 1), ("gB", 2),
         ("gA", 0), ("gA", 1), ("gA", 2), ("gA", 3), ("gB", 3)]
NU = len(UNITS)
GATES = [n for n, (kind, _) in enumerate(UNITS) if kind in ("gA", "gB")]
PLAIN = [n for n in range(NU) if n not in GATES]
PASSES = 3
PIECES = 6
KP = KT * PASSES // PIECES
RAW, SPLIT = 2, 3
XS = 3
WO_RAW = 4
OLDEST = NU % SPLIT
FIRST_PIECES = 24

B_UNITS = B_HEADS * TILES
B_PIECES = [3, 3, 4, 4, 5, 5, 6, 6]
A_PIECES = 3


def slope_a(h):
    return 2.0 ** (-8.0 * (h + 1) / A_HEADS)


def slope_b(h):
    return 2.0 ** (-8.0 * (h + 1) / B_HEADS)


def make_schedule():
    steps, gates = [], []
    pieces = [(n, half, p) for n in range(NU) for half in range(2) for p in range(PIECES)]
    at = 0

    def take(count):
        nonlocal at
        for n, half, p in pieces[at:at + count]:
            if half == 0 and p == 0 and n + 2 < NU:
                steps.append(("split", n + 2))
            steps.append(("project", n, half, p))
            if p == PIECES - 1 and n in GATES:
                gates.append(("gate", n, half))
        at = min(at + count, len(pieces))

    def open_gates():
        steps.extend(gates)
        gates.clear()

    order = [("b", u) for u in range(3 * TILES)] + [("a", c) for c in range(CHUNKS)]
    order += [("b", u) for u in range(3 * TILES, B_UNITS)]
    place = {unit: n for n, unit in enumerate(order)}
    turns = {}
    for unit, n in place.items():
        turns.setdefault(n + (1 if unit[0] == "b" else 2), []).insert(0, unit)

    steps += [("split", 0), ("split", 1)]
    take(FIRST_PIECES)
    for slot in range(len(order) + 3):
        kind, now = order[slot] if slot < len(order) else (None, None)
        count = {"b": B_PIECES[(now or 0) % TILES], "a": A_PIECES, None: 4}[kind]
        last = order[slot - 1] if 0 < slot <= len(order) else (None, None)
        if last[0] == "b":
            steps.append(("b_mix", last[1]))
        before = order[slot - 2] if 2 <= slot < len(order) + 2 else (None, 0)
        finishing = before[0] == "b" and before[1] % 4 == 3
        if finishing:
            steps.append(("b_finish", before[1] // 4))
        if last[0] == "a":
            steps.append(("a_weights", last[1]))
        turning = sorted(turns.get(slot, []))
        for which, unit in turning[:1]:
            steps.append((f"{which}_transpose", unit, 0) if which == "b" else ("a_transpose", unit))
        if kind == "b":
            assert {("kB", now // TILES), ("qB", now // TILES)} <= set(UNITS[:at // (2 * PIECES)])
            steps.append(("b_scores", now))
        elif kind == "a":
            steps.append(("a_scores", now))
        open_gates()
        for n, (which, unit) in enumerate(turning):
            if n:
                steps.append(("b_transpose", unit, 0))
            if which == "b" and unit % TILES >= 4:
                if n or kind is None:
                    take(1)
                    count -= 1
                steps.append(("b_transpose", unit, 1))
            if kind == "b" and n == len(turning) - 1:
                steps.append(("b_exp", now))
            if kind != "a" or which == "b":
                take(1)
                count -= 1
            steps.append((f"{which}_values", unit))
            if which == "b" and unit % 4 == 3:
                steps.append(("b_square", unit // 4))
        if kind == "b" and not turning:
            steps.append(("b_exp", now))
        take(1)
        count -= 1
        open_gates()
        if finishing:
            steps.append(("b_finish_transpose", before[1] // 4))
        take(max(0, count))
    last = (NU - 1) * 2 * PIECES
    outs = list(range(KT))
    while at < len(pieces):
        take(1)
        open_gates()
        if outs and at % 3 == 0:
            steps.append(("split_out", outs.pop(0)))
        if at == last + PIECES + 1:
            steps += [("y_split", 0), ("y_split", 1)]
    steps += [("split_out", k) for k in outs]
    for t in range(TILES):
        if t + 2 < TILES:
            steps.append(("y_split", t + 2))
        steps += [("out_project", t, 0), ("out_project", t, 1), ("post", t)]
    return steps


SCHEDULE = make_schedule()


def order_of(kind, *which):
    same = [s[1:] for s in SCHEDULE if s[0] == kind]
    return same.index(which) + 1


def hybrid_layer(nc, x, w_in, w_out, pre_norm_g, post_norm_g, sinks, lambda_q1, lambda_k1,
                 lambda_q2, lambda_k2, subln_g, out):
    F32, F32R = mybir.dt.float32, mybir.dt.float32r
    ALU, ACT = mybir.AluOpType, mybir.ActivationFunctionType

    base = (nc.sbuf_base + 31) // 32 * 32
    KB = 1024

    def place(name, at_kb, shape, dtype=F32):
        return nc.alloc_sbuf_tensor_at(name, shape, dtype, offset=base + int(at_kb * KB))

    hT_hi = place("hT_hi", 0, [P, KT, SEQ], F32R)
    hT_lo = place("hT_lo", 32, [P, KT, SEQ], F32R)
    w_raw = place("w_raw", 64, [P, RAW, KT, P])
    w_hi = place("w_hi", 72, [P, SPLIT, KT, P], F32R)
    w_lo = place("w_lo", 84, [P, SPLIT, KT, P], F32R)
    v_sb = place("v_sb", 96, [P, TILES, V_WIDTH])
    v_shift = place("v_shift", 116, [P, TILES, P])
    kT_B = place("kT_B", 120, [P, 2, SEQ])
    kT_A = place("kT_A", 128, [P, CHUNK + SEQ])
    weights = place("weights", 132.25, [P, 2, 2, SEQ])
    weightsT = place("weightsT", 148.25, [P, 2, TILES, P])
    a_weights = place("a_weights", 156.25, [P, 2, A_PAIRS, P])
    a_weightsT = place("a_weightsT", 160.25, [P, A_PAIRS, P])
    qT_B = place("qT_B", 162.25, [P, B_HEADS, SEQ])
    qT_A = place("qT_A", 178.25, [P, A_PAIRS, SEQ])
    dist_b = place("dist_b", 194.25, [P, SEQ])
    dist_a = place("dist_a", 198.25, [P, 2, P])
    ident = place("ident", 199.25, [P, P])
    on_b = place("on_b", 199.75, [P, 4, P])
    gate = place("gate", 201.75, [P, 2, HALF])
    junk = place("junk", 205.75, [P, P])
    small = place("small", 206.25, [P, 352])
    wv_raw = place("wv_raw", 120, [P, KT, V_WIDTH])
    x_in = place("x_in", 140, [P, XS, D_MODEL])
    pre_g = place("pre_g", 201.75, [P, D_MODEL])
    wv_hi = place("wv_hi", 152, [P, KT, V_WIDTH], F32R)
    wv_lo = place("wv_lo", 172, [P, KT, V_WIDTH], F32R)
    wo_hi = place("wo_hi", 96, [P, KT, D_MODEL], F32R)
    wo_lo = place("wo_lo", 128, [P, KT, D_MODEL], F32R)
    wo_early = place("wo_early", 72, [P, 2 * SPLIT, D_MODEL])
    post_g = place("post_g", 201.75, [P, D_MODEL])
    x_res = place("x_res", 76, [P, 2, D_MODEL])
    y_out = place("y_out", 88, [P, 2, D_MODEL])

    taken = [0]

    def column(width):
        taken[0] += width
        assert taken[0] <= 352
        return small[:, taken[0] - width:taken[0]]

    x_square = column(TILES)
    x_mean = column(TILES)
    x_scale = column(TILES)
    min_b = column(2 * B_UNITS)
    sum_b = column(2 * B_UNITS)
    inv_b = column(2 * B_UNITS)
    mix_b = column(B_UNITS)
    square_b = column(4)
    mean_b = column(4)
    rms_b = column(4)
    scale_b = column(4)
    min_a = column(2 * A_PAIRS)
    sum_a = column(2 * A_PAIRS)
    sink_arg = column(2 * A_PAIRS)
    sink_w = column(2 * A_PAIRS)
    total_a = column(2 * A_PAIRS)
    inv_a = column(2 * A_PAIRS)
    neg_half = column(4)
    sink = column(A_PAIRS)
    neg_sink = column(A_PAIRS)
    neg_slope = column(A_PAIRS)
    q_scale = column(A_PAIRS)
    sub_g = column(1)
    out_g = column(1)
    lam_dot = column(2)
    lam_exp = column(2)
    lam_dif = column(1)
    neg_lam = column(1)
    lam_in = on_b
    y_square = square_b
    y_mean = mean_b
    y_scale = rms_b

    scores = nc.alloc_psum_tensor("scores", [P, 2048], F32)
    proj = nc.alloc_psum_tensor("proj", [P, 2, HALF], F32)
    banks = nc.alloc_psum_tensor("banks", [P, 1024], F32)
    turned = banks[:, 0:512]
    mixed = banks[:, 512:1024]

    def sem(name):
        return nc.alloc_semaphore(name)

    x_loaded = [sem(f"x_loaded{i}") for i in range(XS)]
    wv_loaded = [sem(f"wv_loaded{i}") for i in range(4)]
    w_loaded = [sem(f"w_loaded{i}") for i in range(RAW)]
    wo_loaded = [sem(f"wo_loaded{i}") for i in range(WO_RAW)]
    pre_g_loaded = sem("pre_g_loaded")
    post_g_loaded = sem("post_g_loaded")
    small_loaded = sem("small_loaded")
    v_shifted = sem("v_shifted")
    res_loaded = [sem("res_loaded0"), sem("res_loaded1")]
    stored = [sem("stored0"), sem("stored1")]
    ident_made = sem("ident_made")
    dist_made = sem("dist_made")
    pads_made = sem("pads_made")
    half_made = sem("half_made")
    consts_made = sem("consts_made")
    slopes_made = sem("slopes_made")
    dist_ready = sem("dist_ready")
    lam_exped = sem("lam_exped")
    x_squared = sem("x_squared")
    x_meaned = sem("x_meaned")
    x_scaled = sem("x_scaled")
    x_normed = sem("x_normed")
    x_turned = sem("x_turned")
    h_hi_ready = sem("h_hi_ready")
    h_lo_ready = sem("h_lo_ready")
    wv_hi_ready = sem("wv_hi_ready")
    wv_lo_ready = sem("wv_lo_ready")
    v_projected = sem("v_projected")
    v_stored = sem("v_stored")
    w_hi_ready = sem("w_hi_ready")
    w_lo_ready = sem("w_lo_ready")
    projected = sem("projected")
    plain_stored = sem("plain_stored")
    tanh_done = sem("tanh_done")
    gate_done = sem("gate_done")
    gated = sem("gated")
    b_scored = sem("b_scored")
    b_biased = sem("b_biased")
    b_exped = sem("b_exped")
    b_inverted = sem("b_inverted")
    b_ratio = sem("b_ratio")
    b_mixed = sem("b_mixed")
    b_valued = sem("b_valued")
    b_squared = sem("b_squared")
    b_meaned = sem("b_meaned")
    b_rooted = sem("b_rooted")
    b_scaled = sem("b_scaled")
    turned_full = sem("turned_full")
    turned_read = sem("turned_read")
    mixed_read = sem("mixed_read")
    a_scored = sem("a_scored")
    a_biased = sem("a_biased")
    a_sinked = sem("a_sinked")
    a_exped = sem("a_exped")
    a_summed = sem("a_summed")
    a_inverted = sem("a_inverted")
    a_weighted = sem("a_weighted")
    a_valued = sem("a_valued")
    wo_hi_ready = sem("wo_hi_ready")
    wo_lo_ready = [sem("wo_lo_ready0"), sem("wo_lo_ready1")]
    y_hi_ready = sem("y_hi_ready")
    y_lo_ready = sem("y_lo_ready")
    out_projected = sem("out_projected")
    y_squared = sem("y_squared")
    y_meaned = sem("y_meaned")
    y_rooted = sem("y_rooted")
    y_normed = sem("y_normed")
    y_added = sem("y_added")

    def halves_done(kind, index, half):
        return 2 * UNITS.index((kind, index)) + half + 1

    def plain_count(kind, index, half):
        return 2 * PLAIN.index(UNITS.index((kind, index))) + half + 1

    turned_users = [s for s in SCHEDULE
                    if s[0] in ("b_transpose", "b_finish_transpose", "a_transpose")]

    def turned_count(*step):
        return turned_users.index(step) + 1

    mixed_users = [s for s in SCHEDULE if s[0] == "a_values" or s[0] == "b_values" and s[1] % 4 == 3]

    def mixed_before(step):
        at = SCHEDULE.index(step)
        return sum(SCHEDULE.index(s) < at for s in mixed_users)

    def gate_count(n, half):
        return 2 * GATES.index(n) + half + 1

    def proj_user(n, half):
        return 2 * TILES + 2 * n + half

    def wait_proj_free(engine, filling):
        before = filling - 2
        if before < 0:
            return
        if before < 2 * TILES:
            engine.wait_ge(v_stored, before + 1)
            return
        n, half = divmod(before - 2 * TILES, 2)
        if n in GATES:
            engine.wait_ge(gate_done, gate_count(n, half))
        else:
            engine.wait_ge(plain_stored, plain_count(*UNITS[n], half))

    w_cols = w_in[0].rearrange("(k p) e -> p k e", p=P)

    def unit_columns(n):
        kind, i = UNITS[n]
        if kind == "kA":
            return [(AK, P)]
        if kind in ("qA", "gA"):
            first = (AQ if kind == "qA" else AG) + HEAD_DIM * i
            return [(first, HEAD_DIM), (first + A_PAIRS * HEAD_DIM, HEAD_DIM)]
        return [({"qB": BQ, "kB": BK, "gB": BG}[kind] + P * i, P)]

    def out_rows(k):
        if k < A_PAIRS:
            return [(HEAD_DIM * k, HEAD_DIM), (HEAD_DIM * (k + A_PAIRS), HEAD_DIM)]
        return [(P * k, P)]

    def load_count(n):
        return sum(16 * len(unit_columns(m)) for m in range(n % RAW, n + 1, RAW))

    def wo_load_count(k):
        return sum(16 * len(out_rows(m)) for m in range(k % WO_RAW, k + 1, WO_RAW))

    def wo_raw(k):
        slot = k % WO_RAW
        return wo_early[:, OLDEST if slot == 0 else SPLIT + OLDEST, :] if slot < 2 else w_raw[:, slot - 2].rearrange("p k c -> p (k c)")

    v_runs = [[(BV, VG, 0)], [(BV + VG, B_WIDTH - VG, VG), (AV, P, B_WIDTH)]]

    with nc.Block() as block:

        @block.sync
        def _(sp):
            def load_x(t):
                if t >= XS:
                    sp.wait_ge(x_turned, t - XS + 1)
                sp.dma_start(x_in[:, t % XS, :], x[0, t * P:(t + 1) * P, :]).then_inc(x_loaded[t % XS], 16)

            load_x(0)
            sp.dma_start(pre_g[:, :], pre_norm_g[0:1, :].to_broadcast([P, D_MODEL])).then_inc(pre_g_loaded, 16)
            for part in range(2):
                k = slice(4 * part, 4 * part + 4)
                sp.dma_start(wv_raw[:, k, 0:VG], w_cols[:, k, BV:BV + VG]).then_inc(wv_loaded[part], 16)
                load_x(part + 1)
            for i, (first, count, to) in enumerate(v_runs[1]):
                sp.dma_start(wv_raw[:, :, to:to + count],
                             w_cols[:, :, first:first + count]).then_inc(wv_loaded[2 + i], 16)
                load_x(3 + i)

            def load_w(n):
                if n >= RAW:
                    sp.wait_ge(w_hi_ready, n - RAW + 1)
                    sp.wait_ge(w_lo_ready, n - RAW + 1)
                to = 0
                for first, count in unit_columns(n):
                    sp.dma_start(w_raw[:, n % RAW, :, to:to + count],
                                 w_cols[:, :, first:first + count]).then_inc(w_loaded[n % RAW], 16)
                    to += count

            def load_wo(k):
                if k < 2:
                    sp.wait_ge(projected, 2 * (NU - SPLIT) + 2)
                elif k < WO_RAW:
                    sp.wait_ge(w_hi_ready, NU)
                    sp.wait_ge(w_lo_ready, NU)
                else:
                    sp.wait_ge(wo_hi_ready, k - WO_RAW + 1)
                    sp.wait_ge(wo_lo_ready[k % 2], (k - WO_RAW) // 2 + 1)
                to = 0
                for first, count in out_rows(k):
                    sp.dma_start(wo_raw(k)[to:to + count, :],
                                 w_out[0, first:first + count, :]).then_inc(wo_loaded[k % WO_RAW], 16)
                    to += count

            load_w(0)
            load_w(1)
            for t in range(5, TILES):
                load_x(t)
            sp.wait_ge(pads_made, 1)
            sp.wait_ge(v_stored, 2 * TILES)
            a_cols = slice(B_WIDTH, V_WIDTH)
            sp.dma_start(v_shift[CHUNK:P, :, :], v_sb[0:CHUNK, :, a_cols]).then_inc(v_shifted, 16)
            sp.dma_start(v_shift[0:CHUNK, 1:TILES, :],
                         v_sb[CHUNK:P, 0:TILES - 1, a_cols]).then_inc(v_shifted, 16)
            for n in range(2, NU):
                load_w(n)
            for k in range(KT):
                load_wo(k)
            sp.wait_ge(projected, 2 * NU)
            sp.wait_ge(gated, 2 * len(GATES))
            sp.dma_start(post_g[:, :], post_norm_g[0:1, :].to_broadcast([P, D_MODEL])).then_inc(post_g_loaded, 16)
            for t in range(TILES):
                if t >= 2:
                    sp.wait_ge(y_added, 2 * t - 2)
                sp.dma_start(x_res[:, t % 2, :], x[0, t * P:(t + 1) * P, :]).then_inc(res_loaded[t % 2], 16)
            for t in range(2):
                sp.wait_ge(stored[t], 16 * 2 * (TILES // 2))

        @block.gpsimd
        def _(pool):
            def low_weights(n):
                pool.wait_ge(w_hi_ready, n + 1)
                nc.gpsimd.tensor_tensor(w_lo[:, n % SPLIT], w_raw[:, n % RAW],
                                        w_hi[:, n % SPLIT].bitcast(F32), ALU.subtract).then_inc(w_lo_ready, 1)

            for h, part in enumerate((slice(0, CHUNK), slice(CHUNK, P))):
                pool.dma_start(sink[part, :], sinks[0:1, 4 * h:4 * h + 4].to_broadcast([CHUNK, 4])).then_inc(small_loaded, 16)
            pool.dma_start(sub_g, subln_g.rearrange("a e -> e a")).then_inc(small_loaded, 16)
            for v, vector in enumerate((lambda_q1, lambda_k1, lambda_q2, lambda_k2)):
                pool.dma_start(lam_in[:, v, 0:HEAD_DIM],
                              vector[0:1, :].to_broadcast([P, HEAD_DIM])).then_inc(small_loaded, 16)
            nc.gpsimd.memset(ident[:, :], 0.0).then_inc(ident_made, 1)
            nc.gpsimd.memset(neg_half, -0.5).then_inc(half_made, 1)
            pool.wait_ge(ident_made, 1)
            nc.gpsimd.affine_select(out=ident[:, :], in_=ident[:, :], compare_op=ALU.not_equal, fill=1.0,
                                    base=0, pattern=[[-1, P]], channel_multiplier=1).then_inc(ident_made, 1)
            nc.gpsimd.iota(dist_b[:, :], [[-1, SEQ]], base=SEQ - P, channel_multiplier=1,
                           allow_small_or_imprecise_dtypes=True).then_inc(dist_made, 1)
            nc.gpsimd.iota(dist_a[:, 1, :], [[-1, P]], base=CHUNK, channel_multiplier=1,
                           allow_small_or_imprecise_dtypes=True).then_inc(dist_made, 1)

            def root(out_, in_, width, done):
                nc.gpsimd.tensor_tensor(out_, in_, neg_half[:, 0:width], ALU.pow).then_inc(done, 1)

            pool.wait_ge(half_made, 1)
            for t in range(TILES):
                pool.wait_ge(x_meaned, t + 1)
                root(x_scale[:, t:t + 1], x_mean[:, t:t + 1], 1, x_scaled)
                if t == TILES - 1:
                    for n in (0, 1):
                        low_weights(n)
            for step, *i in SCHEDULE:
                if step == "split" and i[0] >= 2:
                    low_weights(i[0])
                elif step == "split_out" and i[0] % 2 == 0:
                    k = i[0]
                    pool.wait_ge(wo_hi_ready, k + 1)
                    nc.gpsimd.tensor_tensor(wo_lo[:, k, :], wo_raw(k), wo_hi[:, k, :].bitcast(F32),
                                            ALU.subtract).then_inc(wo_lo_ready[0], 1)
                elif step == "b_square":
                    f = i[0]
                    pool.wait_ge(b_squared, 4 * f + 4)
                    nc.gpsimd.tensor_scalar(mean_b, square_b, 1.0 / P, EPS, ALU.mult, ALU.add).then_inc(b_meaned, 1)
                    pool.wait_ge(b_meaned, f + 1)
                    if f:
                        pool.wait_ge(b_scaled, f)
                    root(rms_b, mean_b, 4, b_rooted)
                elif step == "a_weights":
                    c = i[0]
                    pool.wait_ge(a_inverted, c + 1)
                    w = a_weights[:, c % 2]
                    r = inv_a[:, 4 * (c % 2):4 * (c % 2) + 4].unsqueeze(2).to_broadcast([P, A_PAIRS, P])
                    nc.gpsimd.tensor_tensor(w, w, r, ALU.mult).then_inc(a_weighted, 1)
                elif step == "post":
                    t = i[0]
                    pool.wait_ge(y_meaned, t + 1)
                    root(y_scale[:, t % 2:t % 2 + 1], y_mean[:, t % 2:t % 2 + 1], 1, y_rooted)

        @block.scalar
        def _(act):
            def high_wv(k, cols, ready):
                act.wait_ge(wv_loaded[ready], 16)
                nc.scalar.activation(wv_hi[:, k, cols], wv_raw[:, k, cols], ACT.Copy).then_inc(wv_hi_ready, 1)

            def high_h(t):
                act.wait_ge(x_turned, t + 1)
                nc.scalar.activation(hT_hi[:, :, t * P:(t + 1) * P],
                                     scores[:, 1024 * (t % 2):1024 * (t % 2) + 1024].rearrange("p (k c) -> p k c", c=P),
                                     ACT.Copy).then_inc(h_hi_ready, 1)

            def square_x(t):
                act.wait_ge(x_loaded[t % XS], 16 * (t // XS + 1))
                if t:
                    act.wait_ge(x_squared, t)
                nc.scalar.activation(banks[:, :], x_in[:, t % XS, :], ACT.Square, scale=D_MODEL ** -0.5,
                                     accum_out=x_square[:, t:t + 1]).then_inc(x_squared, 1)

            def store_v(t, g):
                n = TILES * g + t
                act.wait_ge(v_projected, n + 1)
                nc.scalar.activation(v_sb[:, t, VG * g:VG * (g + 1)], proj[:, n % 2, 0:VG],
                                     ACT.Copy).then_inc(v_stored, 1)

            def high_weights(n):
                act.wait_ge(w_loaded[n % RAW], load_count(n))
                if n >= SPLIT:
                    act.wait_ge(projected, 2 * (n - SPLIT) + 2)
                nc.scalar.activation(w_hi[:, n % SPLIT], w_raw[:, n % RAW], ACT.Copy).then_inc(w_hi_ready, 1)

            square_x(0)
            high_wv(slice(0, 4), slice(0, VG), 0)
            square_x(1)
            high_h(0)
            high_wv(slice(4, 8), slice(0, VG), 1)
            for t in range(TILES):
                if t + 2 < TILES:
                    square_x(t + 2)
                if t + 1 < TILES:
                    high_h(t + 1)
                store_v(t, 0)
                if t == 2:
                    high_wv(slice(0, 8), slice(VG, B_WIDTH), 2)
                if t == 3:
                    high_wv(slice(0, 8), slice(B_WIDTH, V_WIDTH), 3)
                if t in (5, 6):
                    high_weights(t - 5)
                if t == 7:
                    act.wait_ge(consts_made, 2)
                    nc.scalar.activation(lam_exp, lam_dot, ACT.Exp).then_inc(lam_exped, 1)
            for t in range(TILES):
                store_v(t, 1)

            for step, *i in SCHEDULE:
                if step == "split" and i[0] >= 2:
                    high_weights(i[0])
                elif step == "split_out":
                    k = i[0]
                    act.wait_ge(wo_loaded[k % WO_RAW], wo_load_count(k))
                    act.wait_ge(turned_full, len(turned_users))
                    nc.scalar.activation(wo_hi[:, k, :], wo_raw(k), ACT.Copy).then_inc(wo_hi_ready, 1)
                elif step == "project" and i[2] == PIECES - 1:
                    n, half, _ = i
                    kind, head = UNITS[n]
                    source = proj[:, proj_user(n, half) % 2, :]
                    tokens = slice(HALF * half, HALF * half + HALF)
                    act.wait_ge(projected, 2 * n + half + 1)
                    if kind == "kB":
                        to = kT_B[:, head % 2, tokens]
                        nc.scalar.activation(to, source, ACT.Copy).then_inc(plain_stored, 1)
                    elif kind == "kA":
                        to = kT_A[:, CHUNK + HALF * half:CHUNK + HALF * half + HALF]
                        nc.scalar.activation(to, source, ACT.Copy).then_inc(plain_stored, 1)
                    elif kind == "qB":
                        nc.scalar.activation(qT_B[:, head, tokens], source, ACT.Copy,
                                             scale=SCALE / slope_b(head)).then_inc(plain_stored, 1)
                    elif kind == "qA":
                        act.wait_ge(slopes_made, 4 * A_PAIRS)
                        nc.scalar.activation(qT_A[:, head, tokens], source, ACT.Copy,
                                             scale=q_scale[:, head:head + 1]).then_inc(plain_stored, 1)
                    else:
                        g = gate_count(n, half) - 1
                        if g >= 2:
                            act.wait_ge(gated, g - 1)
                        nc.scalar.activation(gate[:, g % 2, :], source, ACT.Tanh, scale=0.5).then_inc(tanh_done, 1)
                elif step == "b_exp":
                    u = i[0]
                    keys = P * (u % TILES + 1)
                    for m in range(2):
                        w = weights[:, u % 2, m, 0:keys]
                        act.wait_ge(b_biased, 2 * u + m + 1)
                        nc.scalar.activation(w, w, ACT.Exp, scale=-1.0, bias=min_b[:, 2 * u + m:2 * u + m + 1],
                                             accum_out=sum_b[:, 2 * u + m:2 * u + m + 1]).then_inc(b_exped, 1)
                elif step == "b_transpose":
                    u, r = i
                    blocks = min(4, u % TILES + 1 - 4 * r)
                    if u >= 2:
                        act.wait_ge(b_valued, u - 1)
                    act.wait_ge(turned_full, turned_count("b_transpose", u, r))
                    nc.scalar.activation(weightsT[:, u % 2, 4 * r:4 * r + blocks, :],
                                         turned[:, 0:P * blocks].rearrange("p (b q) -> p b q", q=P),
                                         ACT.Copy).then_inc(turned_read, 1)
                elif step == "b_square":
                    f = i[0]
                    act.wait_ge(b_valued, 4 * f + 4)
                    if f:
                        act.wait_ge(b_meaned, f)
                    for j in range(4):
                        u = 4 * f + j
                        if 4 * f + j:
                            act.wait_ge(b_squared, 4 * f + j)
                        nc.scalar.activation(junk[:, :], mixed[:, P * j:P * j + P], ACT.Square,
                                             scale=inv_b[:, 2 * u:2 * u + 1],
                                             accum_out=square_b[:, j:j + 1]).then_inc(b_squared, 1)
                elif step == "b_finish_transpose":
                    f = i[0]
                    act.wait_ge(turned_full, turned_count("b_finish_transpose", f))
                    act.wait_ge(consts_made, 4)
                    nc.scalar.activation(qT_B[:, f // 2, HALF * (f % 2):HALF * (f % 2) + HALF], turned[:, :],
                                         ACT.Copy, scale=out_g).then_inc(turned_read, 1)
                elif step == "a_scores":
                    c = i[0]
                    s = 4 * (c % 2)
                    for j in range(A_PAIRS):
                        w = a_weights[:, c % 2, j, :]
                        act.wait_ge(a_biased, 4 * c + j + 1)
                        nc.scalar.activation(w, w, ACT.Exp, scale=-1.0, bias=min_a[:, s + j:s + j + 1],
                                             accum_out=sum_a[:, s + j:s + j + 1]).then_inc(a_exped, 1)
                    act.wait_ge(a_sinked, c + 1)
                    nc.scalar.activation(sink_w[:, s:s + 4], sink_arg[:, s:s + 4], ACT.Exp).then_inc(a_exped, 1)
                elif step == "a_transpose":
                    c = i[0]
                    if c:
                        act.wait_ge(a_valued, c)
                    act.wait_ge(turned_full, turned_count("a_transpose", c))
                    nc.scalar.activation(a_weightsT[:, :, :], turned[:, :].rearrange("p (j q) -> p j q", q=P),
                                         ACT.Copy).then_inc(turned_read, 1)
                elif step == "y_split":
                    t = i[0]
                    tokens = slice(P * t, P * t + P)
                    half = t // 4
                    act.wait_ge(projected, 2 * NU - 1 + half)
                    act.wait_ge(gated, 2 * len(GATES) - 1 + half)
                    for first, part in ((0, qT_A), (A_PAIRS, qT_B)):
                        nc.scalar.activation(hT_hi[:, first:first + 4, tokens], part[:, :, tokens],
                                             ACT.Copy).then_inc(y_hi_ready, 1)
                elif step == "out_project":
                    t, half = i
                    act.wait_ge(out_projected, 2 * t + half + 1)
                    if t >= 2:
                        act.wait_ge(y_meaned, t - 1)
                    if 2 * t + half:
                        act.wait_ge(y_squared, 2 * t + half)
                    at = 1024 * (t % 2) + HALF * half
                    nc.scalar.activation(turned, scores[:, at:at + HALF], ACT.Square, scale=D_MODEL ** -0.5,
                                         accum_out=y_square[:, 2 * (t % 2) + half:2 * (t % 2) + half + 1]).then_inc(y_squared, 1)
                elif step == "post":
                    t = i[0]
                    for half in range(2):
                        act.wait_ge(y_added, 2 * t + half + 1)
                        cols = slice(HALF * half, HALF * half + HALF)
                        act.dma_start(out[0, P * t:P * t + P, cols], y_out[:, t % 2, cols]).then_inc(stored[t % 2], 16)

        @block.vector
        def _(dve):
            def mean_x(t):
                dve.wait_ge(x_squared, t + 1)
                nc.vector.tensor_scalar(x_mean[:, t:t + 1], x_square[:, t:t + 1], EPS, None, ALU.add).then_inc(x_meaned, 1)

            def norm_x(t):
                if t == 0:
                    dve.wait_ge(pre_g_loaded, 16)
                dve.wait_ge(x_scaled, t + 1)
                nc.vector.scalar_tensor_tensor(x_in[:, t % XS, :], x_in[:, t % XS, :], x_scale[:, t:t + 1],
                                               pre_g[:, :], ALU.mult, ALU.mult).then_inc(x_normed, 1)

            def low_h(t):
                dve.wait_ge(h_hi_ready, t + 1)
                tokens = slice(P * t, P * t + P)
                s = scores[:, 1024 * (t % 2):1024 * (t % 2) + 1024].rearrange("p (k c) -> p k c", c=P)
                nc.vector.tensor_tensor(hT_lo[:, :, tokens], s, hT_hi[:, :, tokens].bitcast(F32),
                                        ALU.subtract).then_inc(h_lo_ready, 1)

            def low_wv(k, cols, part):
                dve.wait_ge(wv_hi_ready, part + 1)
                nc.vector.tensor_tensor(wv_lo[:, k, cols], wv_raw[:, k, cols], wv_hi[:, k, cols].bitcast(F32),
                                        ALU.subtract).then_inc(wv_lo_ready, 1)

            def constants():
                dve.wait_ge(small_loaded, 16 * 7)
                for d in range(2):
                    a, b = (lam_in[:, v, 0:HEAD_DIM] for v in (2 * d, 2 * d + 1))
                    nc.vector.tensor_tensor_reduce(out=junk[:, HEAD_DIM * d:HEAD_DIM * (d + 1)], in0=a, in1=b, scale=1.0, scalar=0.0,
                                                   op0=ALU.mult, op1=ALU.add,
                                                   accum_out=lam_dot[:, d:d + 1]).then_inc(consts_made, 1)
                nc.vector.tensor_scalar(neg_sink, sink, -1.0, None, ALU.mult).then_inc(consts_made, 1)
                nc.vector.tensor_scalar(out_g, sub_g, 0.5 * (1.0 - LAMBDA_INIT), None, ALU.mult).then_inc(consts_made, 1)
                for j in range(A_PAIRS):
                    for h, part in ((j, slice(0, CHUNK)), (j + A_PAIRS, slice(CHUNK, P))):
                        nc.vector.memset(q_scale[part, j:j + 1], SCALE / slope_a(h)).then_inc(slopes_made, 1)
                        nc.vector.memset(neg_slope[part, j:j + 1], -slope_a(h)).then_inc(slopes_made, 1)
                nc.vector.memset(v_shift[0:CHUNK, 0, :], 0.0).then_inc(pads_made, 1)
                dve.wait_ge(dist_made, 2)
                lower = dist_a[CHUNK:P, 1, :]
                nc.vector.tensor_scalar(lower, lower, float(CHUNK), None, ALU.subtract).then_inc(dist_ready, 1)
                dve.wait_ge(dist_ready, 1)
                for d in (dist_b[:, :], dist_a[:, 1, :]):
                    nc.vector.scalar_tensor_tensor(d, d, -1.0, d, ALU.mult, ALU.min).then_inc(dist_ready, 1)
                dve.wait_ge(dist_ready, 3)
                nc.vector.memset(dist_b[0:CHUNK, SEQ - CHUNK:SEQ], MASKED).then_inc(dist_ready, 1)
                nc.vector.tensor_copy(dist_a[:, 0, CHUNK:P], dist_a[:, 1, CHUNK:P]).then_inc(dist_ready, 1)
                nc.vector.memset(dist_a[:, 0, 0:CHUNK], MASKED).then_inc(dist_ready, 1)

            def make_lambda():
                dve.wait_ge(lam_exped, 1)
                nc.vector.tensor_tensor(lam_dif, lam_exp[:, 1:2], lam_exp[:, 0:1], ALU.subtract).then_inc(consts_made, 1)
                dve.wait_ge(consts_made, 5)
                nc.vector.tensor_scalar(neg_lam, lam_dif, LAMBDA_INIT, None, ALU.subtract).then_inc(consts_made, 1)

            mean_x(0)
            norm_x(0)
            low_wv(slice(0, 4), slice(0, VG), 0)
            mean_x(1)
            norm_x(1)
            low_h(0)
            low_wv(slice(4, 8), slice(0, VG), 1)
            for t in range(TILES):
                if t + 2 < TILES:
                    mean_x(t + 2)
                    norm_x(t + 2)
                if t + 1 < TILES:
                    low_h(t + 1)
                if t == 2:
                    low_wv(slice(0, 8), slice(VG, B_WIDTH), 2)
                if t == 3:
                    low_wv(slice(0, 8), slice(B_WIDTH, V_WIDTH), 3)
                if t == 5:
                    constants()
            make_lambda()
            dve.wait_ge(v_projected, 2 * TILES)
            nc.vector.memset(kT_A[:, 0:CHUNK], 0.0).then_inc(pads_made, 1)
            dve.wait_ge(dist_ready, 6)

            for step, *i in SCHEDULE:
                if step == "gate":
                    n, half = i
                    kind, head = UNITS[n]
                    g = gate_count(n, half) - 1
                    tokens = slice(HALF * half, HALF * half + HALF)
                    source = proj[:, proj_user(n, half) % 2, :]
                    o = (qT_A if kind == "gA" else qT_B)[:, head, tokens]
                    dve.wait_ge(tanh_done, g + 1)
                    nc.vector.scalar_tensor_tensor(gate[:, g % 2, :], gate[:, g % 2, :], 1.0, source,
                                                   ALU.add, ALU.mult).then_inc(gate_done, 1)
                    dve.wait_ge(gate_done, g + 1)
                    if kind == "gB":
                        dve.wait_ge(turned_read, turned_count("b_finish_transpose", 2 * head + half))
                    else:
                        dve.wait_ge(mixed_read, mixed_users.index(("a_values", CHUNKS - 1)) + 1)
                    nc.vector.tensor_tensor(o, gate[:, g % 2, :], o, ALU.mult).then_inc(gated, 1)
                elif step == "split_out" and i[0] % 2 == 1:
                    k = i[0]
                    dve.wait_ge(wo_hi_ready, k + 1)
                    nc.vector.tensor_tensor(wo_lo[:, k, :], wo_raw(k), wo_hi[:, k, :].bitcast(F32),
                                            ALU.subtract).then_inc(wo_lo_ready[1], 1)
                elif step == "b_mix":
                    u = i[0]
                    keys = P * (u % TILES + 1)
                    dve.wait_ge(b_exped, 2 * u + 2)
                    pair = slice(2 * u, 2 * u + 2)
                    nc.vector.reciprocal(inv_b[:, pair], sum_b[:, pair]).then_inc(b_inverted, 1)
                    dve.wait_ge(b_inverted, u + 1)
                    nc.vector.tensor_scalar(mix_b[:, u:u + 1], sum_b[:, 2 * u:2 * u + 1], inv_b[:, 2 * u + 1:2 * u + 2],
                                            neg_lam, ALU.mult, ALU.mult).then_inc(b_ratio, 1)
                    dve.wait_ge(b_ratio, u + 1)
                    w0, w1 = (weights[:, u % 2, m, 0:keys] for m in range(2))
                    nc.vector.scalar_tensor_tensor(w0, w1, mix_b[:, u:u + 1], w0, ALU.mult, ALU.add).then_inc(b_mixed, 1)
                elif step == "b_scores":
                    u = i[0]
                    keys = P * (u % TILES + 1)
                    if u >= 2:
                        dve.wait_ge(turned_full, turned_count("b_transpose", u - 2, ((u - 2) % TILES) // 4))
                        dve.wait_ge(b_mixed, u - 1)
                    for m in range(2):
                        dve.wait_ge(b_scored, 2 * u + m + 1)
                        nc.vector.tensor_tensor_reduce(
                            out=weights[:, u % 2, m, 0:keys], in0=scores[:, 1024 * m:1024 * m + keys],
                            in1=dist_b[:, SEQ - keys:SEQ], scale=-slope_b(u // TILES), scalar=-MASKED,
                            op0=ALU.add, op1=ALU.min,
                            accum_out=min_b[:, 2 * u + m:2 * u + m + 1]).then_inc(b_biased, 1)
                elif step == "b_finish":
                    f = i[0]
                    dve.wait_ge(b_rooted, f + 1)
                    nc.vector.tensor_tensor(scale_b, rms_b, inv_b[:, 8 * f:8 * f + 8].rearrange("p (u m) -> p u m", m=2)[:, :, 0],
                                            ALU.mult).then_inc(b_scaled, 1)
                    dve.wait_ge(b_scaled, f + 1)
                    if f:
                        dve.wait_ge(turned_full, turned_count("b_finish_transpose", f - 1))
                    nc.vector.tensor_tensor(on_b[:, :, :], mixed.rearrange("p (u e) -> p u e", e=P),
                                            scale_b.unsqueeze(2).to_broadcast([P, 4, P]), ALU.mult).then_inc(mixed_read, 1)
                elif step == "a_scores":
                    c = i[0]
                    s = 4 * (c % 2)
                    if c == 0:
                        dve.wait_ge(slopes_made, 4 * A_PAIRS)
                    if c >= 2:
                        dve.wait_ge(turned_full, turned_count("a_transpose", c - 2))
                    dve.wait_ge(a_scored, c + 1)
                    for j in range(A_PAIRS):
                        nc.vector.tensor_tensor_reduce(
                            out=a_weights[:, c % 2, j, :], in0=scores[:, 512 * (c % 4) + P * j:512 * (c % 4) + P * (j + 1)],
                            in1=dist_a[:, min(c, 1), :], scale=neg_slope[:, j:j + 1], scalar=neg_sink[:, j:j + 1],
                            op0=ALU.add, op1=ALU.min, accum_out=min_a[:, s + j:s + j + 1]).then_inc(a_biased, 1)
                    dve.wait_ge(a_biased, 4 * c + 4)
                    nc.vector.tensor_tensor(sink_arg[:, s:s + 4], min_a[:, s:s + 4], sink, ALU.add).then_inc(a_sinked, 1)
                elif step == "a_weights":
                    c = i[0]
                    s = 4 * (c % 2)
                    dve.wait_ge(a_exped, 5 * c + 5)
                    nc.vector.tensor_tensor(total_a[:, s:s + 4], sum_a[:, s:s + 4], sink_w[:, s:s + 4], ALU.add).then_inc(a_summed, 1)
                    dve.wait_ge(a_summed, c + 1)
                    nc.vector.reciprocal(inv_a[:, s:s + 4], total_a[:, s:s + 4]).then_inc(a_inverted, 1)
                elif step == "a_values":
                    c = i[0]
                    dve.wait_ge(a_valued, c + 1)
                    nc.vector.tensor_scalar(qT_A[:, :, CHUNK * c:CHUNK * c + CHUNK],
                                            mixed[:, 0:A_PAIRS * CHUNK].rearrange("p (j q) -> p j q", q=CHUNK),
                                            0.5, None, ALU.mult).then_inc(mixed_read, 1)
                elif step == "y_split":
                    t = i[0]
                    tokens = slice(P * t, P * t + P)
                    for p, (first, part) in enumerate(((0, qT_A), (A_PAIRS, qT_B))):
                        dve.wait_ge(y_hi_ready, 2 * t + p + 1)
                        nc.vector.tensor_tensor(hT_lo[:, first:first + 4, tokens], part[:, :, tokens],
                                                hT_hi[:, first:first + 4, tokens].bitcast(F32),
                                                ALU.subtract).then_inc(y_lo_ready, 1)
                elif step == "post":
                    t = i[0]
                    dve.wait_ge(y_squared, 2 * t + 2)
                    s = 2 * (t % 2)
                    nc.vector.scalar_tensor_tensor(y_mean[:, t % 2:t % 2 + 1], y_square[:, s:s + 1], EPS,
                                                   y_square[:, s + 1:s + 2], ALU.add, ALU.add).then_inc(y_meaned, 1)
                    if t == 0:
                        dve.wait_ge(post_g_loaded, 16)
                    if t >= 2:
                        dve.wait_ge(stored[t % 2], 32 * (t // 2))
                    dve.wait_ge(y_rooted, t + 1)
                    for half in range(2):
                        cols = slice(HALF * half, HALF * half + HALF)
                        at = 1024 * (t % 2) + HALF * half
                        nc.vector.scalar_tensor_tensor(y_out[:, t % 2, cols], scores[:, at:at + HALF],
                                                       y_scale[:, t % 2:t % 2 + 1], post_g[:, cols],
                                                       ALU.mult, ALU.mult).then_inc(y_normed, 1)
                    dve.wait_ge(res_loaded[t % 2], 16 * (t // 2 + 1))
                    for half in range(2):
                        cols = slice(HALF * half, HALF * half + HALF)
                        dve.wait_ge(y_normed, 2 * t + half + 1)
                        nc.vector.tensor_tensor(y_out[:, t % 2, cols], y_out[:, t % 2, cols],
                                                x_res[:, t % 2, cols], ALU.add).then_inc(y_added, 1)

        @block.tensor
        def _(pe):
            def turn_x(t):
                pe.wait_ge(x_normed, t + 1)
                if t >= 2:
                    pe.wait_ge(h_lo_ready, t - 1)
                for k in range(KT):
                    at = 1024 * (t % 2) + P * k
                    last = nc.tensor.transpose(scores[:, at:at + P], x_in[:, t % XS, P * k:P * k + P], ident[:, :])
                last.then_inc(x_turned, 1)

            def project_v(t, g):
                n = TILES * g + t
                wait_proj_free(pe, n)
                pe.wait_ge(h_lo_ready, t + 1)
                pe.wait_ge(wv_lo_ready, 2 * g + 2)
                tokens, cols = slice(P * t, P * t + P), slice(VG * g, VG * (g + 1))
                for p, (h, w) in enumerate(((hT_hi, wv_hi), (hT_lo, wv_hi), (hT_hi, wv_lo))):
                    for k in range(KT):
                        last = nc.tensor.matmul(proj[:, n % 2, 0:VG], h[:, k, tokens], w[:, k, cols],
                                                start=(p == 0 and k == 0), stop=(p == PASSES - 1 and k == KT - 1))
                last.then_inc(v_projected, 1)

            pe.wait_ge(ident_made, 2)
            turn_x(0)
            turn_x(1)
            for t in range(TILES):
                project_v(t, 0)
                if t + 2 < TILES:
                    turn_x(t + 2)
            for t in range(TILES):
                project_v(t, 1)

            for step, *i in SCHEDULE:
                if step == "project":
                    n, half, p = i
                    to = proj[:, proj_user(n, half) % 2, :]
                    slot = n % SPLIT
                    if p == 0:
                        wait_proj_free(pe, proj_user(n, half))
                        pe.wait_ge(w_hi_ready, n + 1)
                    which, first = divmod(p * KP, KT)
                    if which == PASSES - 1:
                        pe.wait_ge(w_lo_ready, n + 1)
                    w, h = ((w_hi, hT_hi), (w_hi, hT_lo), (w_lo, hT_hi))[which]
                    for k in range(first, first + KP):
                        last = nc.tensor.matmul(to, w[:, slot, k, :], h[:, k, HALF * half:HALF * half + HALF],
                                                start=(p == 0 and k == first),
                                                stop=(p == PIECES - 1 and k == KT - 1))
                    if p == PIECES - 1:
                        last.then_inc(projected, 1)
                elif step == "b_scores":
                    u = i[0]
                    head, block_ = divmod(u, TILES)
                    keys = P * (block_ + 1)
                    pe.wait_ge(plain_stored, plain_count("qB", head, block_ // 4))
                    if u == 3 * TILES:
                        pe.wait_ge(a_biased, A_PAIRS * CHUNKS)
                    for m in range(2):
                        if u:
                            pe.wait_ge(b_biased, 2 * u - 1 + m)
                        part = slice(HEAD_DIM * m, HEAD_DIM * (m + 1))
                        for first in range(0, keys, HALF):
                            width = min(HALF, keys - first)
                            last = nc.tensor.matmul(scores[:, 1024 * m + first:1024 * m + first + width],
                                                    qT_B[part, head, P * block_:P * block_ + P],
                                                    kT_B[part, head % 2, first:first + width], start=True, stop=True)
                        last.then_inc(b_scored, 1)
                elif step == "b_transpose":
                    u, r = i
                    pe.wait_ge(b_mixed, u + 1)
                    pe.wait_ge(turned_read, turned_count("b_transpose", u, r) - 1) if turned_count("b_transpose", u, r) > 1 else None
                    for b in range(4 * r, min(4 * r + 4, u % TILES + 1)):
                        last = nc.tensor.transpose(turned[:, P * (b - 4 * r):P * (b - 4 * r) + P],
                                                   weights[:, u % 2, 0, P * b:P * b + P], ident[:, :])
                    last.then_inc(turned_full, 1)
                elif step == "b_values":
                    u = i[0]
                    head, blocks = u // TILES, u % TILES + 1
                    pe.wait_ge(turned_read, turned_count("b_transpose", u, (blocks - 1) // 4))
                    if u % 4 == 0 and mixed_before((step, *i)):
                        pe.wait_ge(mixed_read, mixed_before((step, *i)))
                    for b in range(blocks):
                        last = nc.tensor.matmul(mixed[:, P * (u % 4):P * (u % 4) + P], weightsT[:, u % 2, b, :],
                                                v_sb[:, b, P * head:P * head + P], start=(b == 0), stop=(b == blocks - 1))
                    last.then_inc(b_valued, 1)
                elif step == "b_finish_transpose":
                    f = i[0]
                    pe.wait_ge(mixed_read, mixed_users.index(("b_values", 4 * f + 3)) + 1)
                    pe.wait_ge(turned_read, turned_count(step, f) - 1)
                    for j in range(4):
                        last = nc.tensor.transpose(turned[:, P * j:P * j + P], on_b[:, j, :], ident[:, :])
                    last.then_inc(turned_full, 1)
                elif step == "a_scores":
                    c = i[0]
                    if c == 0:
                        pe.wait_ge(pads_made, 2)
                        pe.wait_ge(v_shifted, 32)
                        pe.wait_ge(plain_stored, plain_count("qA", A_PAIRS - 1, 1))
                        pe.wait_ge(b_biased, 2 * 3 * TILES)
                    if c >= 4:
                        pe.wait_ge(a_biased, A_PAIRS * (c - 3))
                    for j in range(A_PAIRS):
                        for h in range(2):
                            part = slice(HEAD_DIM * h, HEAD_DIM * (h + 1))
                            at = 512 * (c % 4) + P * j
                            last = nc.tensor.matmul(scores[part, at:at + P], qT_A[part, j, CHUNK * c:CHUNK * c + CHUNK],
                                                    kT_A[part, CHUNK * c:CHUNK * c + P], start=True, stop=True)
                    last.then_inc(a_scored, 1)
                elif step == "a_transpose":
                    c = i[0]
                    pe.wait_ge(a_weighted, c + 1)
                    pe.wait_ge(turned_read, turned_count(step, c) - 1)
                    for j in range(A_PAIRS):
                        last = nc.tensor.transpose(turned[:, P * j:P * j + P], a_weights[:, c % 2, j, :], ident[:, :])
                    last.then_inc(turned_full, 1)
                elif step == "a_values":
                    c = i[0]
                    pe.wait_ge(turned_read, turned_count("a_transpose", c))
                    pe.wait_ge(mixed_read, mixed_before((step, *i)))
                    for h in range(2):
                        part = slice(HEAD_DIM * h, HEAD_DIM * (h + 1))
                        v = v_sb[:, c // 2, B_WIDTH:V_WIDTH] if c % 2 else v_shift[:, c // 2, :]
                        last = nc.tensor.matmul(mixed[part, 0:A_PAIRS * CHUNK], v[:, part],
                                                a_weightsT[:, :, part], start=True, stop=True)
                    last.then_inc(a_valued, 1)
                elif step == "out_project":
                    t, half = i
                    tokens, cols = slice(P * t, P * t + P), slice(HALF * half, HALF * half + HALF)
                    pe.wait_ge(y_lo_ready, 2 * t + 2)
                    if t >= 2:
                        pe.wait_ge(y_normed, 2 * (t - 2) + half + 1)
                    at = 1024 * (t % 2) + HALF * half
                    for p, (y, w) in enumerate(((hT_hi, wo_hi), (hT_lo, wo_hi), (hT_hi, wo_lo))):
                        for k in range(KT):
                            if t == 0 and half == 0 and p != 1:
                                if p:
                                    pe.wait_ge(wo_lo_ready[k % 2], k // 2 + 1)
                                else:
                                    pe.wait_ge(wo_hi_ready, k + 1)
                            last = nc.tensor.matmul(scores[:, at:at + HALF], y[:, k, tokens], w[:, k, cols],
                                                    start=(p == 0 and k == 0), stop=(p == PASSES - 1 and k == KT - 1))
                    last.then_inc(out_projected, 1)


INPUTS = ["x", "w_in", "w_out", "pre_norm_g", "post_norm_g", "sinks", "lambda_q1", "lambda_k1",
          "lambda_q2", "lambda_k2", "subln_g"]


def kernel(**inputs):
    import concourse.bacc as bacc
    import numpy as np
    from concourse.bass_utils import run_bass_kernel_spmd

    nc = bacc.Bacc("TRN2", target_bir_lowering=False, num_devices=1)
    arrays = {f"in_{name}": np.ascontiguousarray(inputs[name]) for name in INPUTS}
    args = [nc.dram_tensor(name, a.shape, mybir.dt.from_np(a.dtype), kind="ExternalInput").ap()
            for name, a in arrays.items()]
    out = nc.dram_tensor("out", (1, SEQ, D_MODEL), mybir.dt.float32, kind="ExternalOutput").ap()
    hybrid_layer(nc, *args, out)
    result = run_bass_kernel_spmd(nc, [arrays], core_ids=[0])
    return result.results[0]["out"]
```

```python
import math

import concourse.bass as bass
from concourse import mybir

P = 128
SEQ, D_MODEL = 1024, 1024
CHUNK, HEAD_DIM = 64, 64
EPS = 1e-6
MASKED = -1e30
A_HEADS, A_KV = 8, 2
A_PAIRS = A_HEADS // A_KV
A_WIDTH = A_HEADS * HEAD_DIM
B_HEADS, B_WIDTH = 4, 512
TILES = SEQ // P
KT = D_MODEL // P
CHUNKS = SEQ // CHUNK
HALF = 512
LAMBDA_INIT = 0.8 - 0.6 * math.exp(-0.3 * 0)
SCALE = 1.0 / math.sqrt(HEAD_DIM)

AQ, AK = 0, A_WIDTH
AV = AK + A_KV * HEAD_DIM
AG = AV + A_KV * HEAD_DIM
BQ = AG + A_WIDTH
BK = BQ + B_WIDTH
BV = BK + B_WIDTH
BG = BV + B_WIDTH
V_WIDTH = B_WIDTH + A_KV * HEAD_DIM
VG = V_WIDTH // 2

UNITS = [("qB", 0), ("kB", 0), ("qB", 1), ("kA", 0), ("kB", 1), ("qB", 2), ("qA", 0), ("kB", 2),
         ("qA", 1), ("qA", 2), ("qA", 3), ("qB", 3), ("kB", 3), ("gB", 0), ("gB", 1), ("gB", 2),
         ("gA", 0), ("gA", 1), ("gA", 2), ("gA", 3), ("gB", 3)]
NU = len(UNITS)
GATES = [n for n, (kind, _) in enumerate(UNITS) if kind in ("gA", "gB")]
PLAIN = [n for n, (kind, _) in enumerate(UNITS) if kind in ("qA", "kA")]
STACKED = [n for n, (kind, _) in enumerate(UNITS) if kind in ("qB", "kB")]
B_ORDER = [0, 2, 1, 3]
PASSES = 3
PIECES = 6
KP = KT * PASSES // PIECES
RAW, SPLIT = 2, 3
XS = 3
WARM_UP = 24
WV_AT = 5
Y_PARTS = 3
WO_RAW = 4
OLDEST = NU % SPLIT
FIRST_PIECES = 24

B_UNITS = B_HEADS * TILES
PIECES_BESIDE = ([9, 4, 3, 4, 4, 5, 3, 7] + [5, 5, 2, 3, 6, 5, 2, 8] + [5, 5, 3, 4, 3, 5, 3, 6]
                 + [5, 3, 3, 1, 1, 4, 3, 4, 3, 2, 2, 4, 3, 2, 3, 2]
                 + [4, 7, 7, 6, 3, 6, 5, 5] + [6, 1, 5])
SCORES_FIRST = {1, 2, 3, 10, 11, 17, 18, 45}
PIECE_BETWEEN = {16, 27, 31, 44, 45}
A_BEFORE = 1
OUT_EVERY = 2


def slope_a(h):
    return 2.0 ** (-8.0 * (h + 1) / A_HEADS)


def slope_b(h):
    return 2.0 ** (-8.0 * (h + 1) / B_HEADS)


def make_schedule():
    steps, later, held = [], [], []
    pieces = [(n, half, p) for n in range(NU) for half in range(2) for p in range(PIECES)]
    at = 0

    def take(count):
        nonlocal at
        for n, half, p in pieces[at:at + count]:
            if half == 0 and p == 0 and n + 2 < NU:
                steps.append(("split", n + 2))
            steps.append(("project", n, half, p))
            if p < PIECES - 1:
                continue
            kind, head = UNITS[n]
            if kind == "kB" and head and ("b_scores", head * TILES - 1) not in steps:
                held.append((n, half))
            else:
                store(n, half)
        at = min(at + count, len(pieces))

    def store(n, half):
        steps.append(("store", n, half))
        if n not in PLAIN:
            later.append(("gate" if n in GATES else "store_low", n, half))

    def vector_parts():
        steps.extend(later)
        later.clear()

    order = [("b", u) for u in range(3 * TILES)] + [("a", c) for c in range(CHUNKS)]
    order += [("b", u) for u in range(3 * TILES, B_UNITS)]
    place = {unit: n for n, unit in enumerate(order)}
    turns = {}
    for unit, n in place.items():
        turns.setdefault(n + (1 if unit[0] == "b" else 2), []).insert(0, unit)

    steps += [("split", 0), ("split", 1)]
    take(FIRST_PIECES)
    vector_parts()
    for slot in range(len(order) + 3):
        kind, now = order[slot] if slot < len(order) else (None, None)
        count = PIECES_BESIDE[slot]
        last = order[slot - 1] if 0 < slot <= len(order) else (None, None)
        if last[0] == "b":
            steps.append(("b_mix", last[1]))
        before = order[slot - 2] if 2 <= slot < len(order) + 2 else (None, 0)
        finishing = before[0] == "b" and before[1] % 4 == 3
        if finishing:
            steps.append(("b_finish", before[1] // 4))
        if last[0] == "a":
            steps.append(("a_weights", last[1]))
        turning = sorted(turns.get(slot, []))
        first = [(f"{which}_transpose", unit, 0) if which == "b" else ("a_transpose", unit)
                 for which, unit in turning[:1]]
        if kind == "b":
            assert {("kB", now // TILES), ("qB", now // TILES)} <= set(UNITS[:at // (2 * PIECES)])
            first.append(("b_scores", now))
        elif kind == "a":
            first.append(("a_scores", now))
        if slot in SCORES_FIRST:
            first.reverse()
        steps += first[:1]
        if slot in PIECE_BETWEEN and len(first) == 2:
            take(1)
            count -= 1
        steps += first[1:]
        vector_parts()
        for n, (which, unit) in enumerate(turning):
            if n:
                steps.append(("b_transpose", unit, 0))
            if which == "b" and unit % TILES >= 4:
                if n or kind is None:
                    take(1)
                    count -= 1
                steps.append(("b_transpose", unit, 1))
            if kind == "b" and n == len(turning) - 1:
                if now % TILES == TILES - 1:
                    for later_n, half in held:
                        store(later_n, half)
                    held.clear()
                steps.append(("b_exp", now))
            now_taken = min(count, A_BEFORE) if kind == "a" and which == "a" else 1 + finishing
            take(now_taken)
            count -= now_taken
            steps.append((f"{which}_values", unit))
            if which == "b" and unit % 4 == 3:
                steps.append(("b_square", unit // 4))
        if kind == "b" and not turning:
            steps.append(("b_exp", now))
        take(1)
        count -= 1
        vector_parts()
        if finishing:
            steps.append(("b_finish_transpose", before[1] // 4))
        take(max(0, count))
    last = (NU - 1) * 2 * PIECES
    outs = list(range(KT))
    while at < len(pieces):
        take(1)
        vector_parts()
        if outs and at % OUT_EVERY == 0:
            steps.append(("split_out", outs.pop(0)))
        if at == last + PIECES + 1:
            steps += [("y_split", 0), ("y_split", 1)]
    steps += [("split_out", k) for k in outs]
    for t in range(TILES):
        if t + 2 < TILES:
            steps.append(("y_split", t + 2))
        steps += [("out_project", t, 0), ("out_project", t, 1), ("post", t)]
    return steps


SCHEDULE = make_schedule()


def hybrid_layer(nc, x, w_in, w_out, pre_norm_g, post_norm_g, sinks, lambda_q1, lambda_k1,
                 lambda_q2, lambda_k2, subln_g, out):
    F32, F32R = mybir.dt.float32, mybir.dt.float32r
    ALU, ACT = mybir.AluOpType, mybir.ActivationFunctionType

    base = (nc.sbuf_base + 31) // 32 * 32
    KB = 1024

    def place(name, at_kb, shape, dtype=F32):
        return nc.alloc_sbuf_tensor_at(name, shape, dtype, offset=base + int(at_kb * KB))

    hT_hi = place("hT_hi", 0, [P, KT, SEQ], F32R)
    hT_lo = place("hT_lo", 32, [P, KT, SEQ], F32R)
    w_raw = place("w_raw", 64, [P, RAW, KT, P])
    w_hi = place("w_hi", 72, [P, SPLIT, KT, P], F32R)
    w_lo = place("w_lo", 84, [P, SPLIT, KT, P], F32R)
    v_sb = place("v_sb", 96, [P, TILES, V_WIDTH])
    v_shift = place("v_shift", 116, [P, TILES, P])
    k_stack = place("k_stack", 120, [P, 2, 2, SEQ], F32R)
    k_hi, k_lo = k_stack[:, 0], k_stack[:, 1]
    kT_A = place("kT_A", 136, [P, CHUNK + SEQ])
    weights_0 = place("weights_0", 140.25, [P, 2, SEQ])
    weights_1 = place("weights_1", 148.25, [P, SEQ])
    weightsT = place("weightsT", 152.25, [P, TILES, P])
    a_weights = place("a_weights", 148.25, [P, 2, A_PAIRS, P])
    a_weightsT = place("a_weightsT", 152.25, [P, A_PAIRS, P])
    q_places = [164.25, 168.25, 172.25, 176.25, 156.25, 160.25]
    q_stack = [[place(f"q_stack{h}{m}", q_places[b], [P, SEQ], F32R) for m, b in enumerate(pair)]
               for h, pair in enumerate([(0, 1), (2, 3), (1, 4), (3, 5)])]
    out_B = place("out_B", 164.25, [P, B_HEADS, SEQ])
    qT_A = place("qT_A", 180.25, [P, 2, CHUNKS, 2, CHUNK])
    dist_b = place("dist_b", 196.25, [P, SEQ])
    dist_a = place("dist_a", 200.25, [P, 2, P])
    ident = place("ident", 201.25, [P, P])
    on_b = place("on_b", 201.75, [P, 4, P])
    gate = place("gate", 203.75, [P, HALF])
    junk = place("junk", 205.75, [P, P])
    small = place("small", 206.25, [P, 352])
    wv_raw = place("wv_raw", 120, [P, KT, V_WIDTH])
    x_in = place("x_in", 140, [P, XS, D_MODEL])
    wv_hi = place("wv_hi", 152, [P, KT, V_WIDTH], F32R)
    wv_lo = place("wv_lo", 172, [P, KT, V_WIDTH], F32R)
    pre_g = place("pre_g", 201.75, [P, D_MODEL])
    lam_in = place("lam_in", 118, [P, 4, HEAD_DIM])
    wo_hi = place("wo_hi", 96, [P, KT, D_MODEL], F32R)
    wo_lo = place("wo_lo", 128, [P, KT, D_MODEL], F32R)
    wo_early = place("wo_early", 72, [P, 2 * SPLIT, D_MODEL])
    post_g = place("post_g", 201.75, [P, D_MODEL])
    x_res = place("x_res", 76, [P, 2, D_MODEL])
    y_out = place("y_out", 88, [P, 2, D_MODEL])

    taken = [0]

    def column(width):
        taken[0] += width
        assert taken[0] <= 352
        return small[:, taken[0] - width:taken[0]]

    x_square = column(TILES)
    x_mean = column(TILES)
    x_scale = column(TILES)
    min_b = column(2 * B_UNITS)
    sum_b = column(2 * B_UNITS)
    inv_b = column(2 * B_UNITS)
    mix_b = column(B_UNITS)
    square_b = column(4)
    mean_b = column(4)
    rms_b = column(4)
    scale_b = column(4)
    min_a = column(2 * A_PAIRS)
    sum_a = column(2 * A_PAIRS)
    sink_arg = column(2 * A_PAIRS)
    sink_w = column(2 * A_PAIRS)
    total_a = column(2 * A_PAIRS)
    inv_a = column(2 * A_PAIRS)
    neg_half = column(4)
    sink_in = column(A_HEADS)
    neg_sink = column(A_PAIRS)
    neg_slope = column(A_PAIRS)
    q_scale = column(A_PAIRS)
    sub_g = column(1)
    out_g = column(1)
    lam_dot = column(2)
    lam_exp = column(2)
    lam_dif = column(1)
    neg_lam = column(1)
    y_square = square_b
    y_mean = mean_b
    y_scale = rms_b

    scores = nc.alloc_psum_tensor("scores", [P, 2048], F32)
    proj = nc.alloc_psum_tensor("proj", [P, 2, HALF], F32)
    banks = nc.alloc_psum_tensor("banks", [P, 1024], F32)
    turned = banks[:, 0:512]
    mixed = banks[:, 512:1024]

    def sem(name):
        return nc.alloc_semaphore(name)

    x_loaded = [sem(f"x_loaded{i}") for i in range(XS)]
    wv_loaded = [sem(f"wv_loaded{i}") for i in range(4)]
    w_loaded = [sem(f"w_loaded{i}") for i in range(RAW)]
    wo_loaded = [sem(f"wo_loaded{i}") for i in range(WO_RAW)]
    pre_g_loaded = sem("pre_g_loaded")
    post_g_loaded = sem("post_g_loaded")
    small_loaded = sem("small_loaded")
    v_shifted = sem("v_shifted")
    res_loaded = [sem("res_loaded0"), sem("res_loaded1")]
    stored = [sem("stored0"), sem("stored1")]
    ident_made = sem("ident_made")
    dist_made = sem("dist_made")
    pads_made = sem("pads_made")
    half_made = sem("half_made")
    consts_made = sem("consts_made")
    slopes_made = sem("slopes_made")
    dist_ready = sem("dist_ready")
    lam_exped = sem("lam_exped")
    x_squared = sem("x_squared")
    x_meaned = sem("x_meaned")
    x_scaled = sem("x_scaled")
    x_normed = sem("x_normed")
    x_turned = sem("x_turned")
    h_hi_ready = sem("h_hi_ready")
    h_lo_ready = sem("h_lo_ready")
    wv_hi_ready = sem("wv_hi_ready")
    wv_lo_first = sem("wv_lo_first")
    wv_lo_ready = sem("wv_lo_ready")
    v_projected = sem("v_projected")
    v_stored = sem("v_stored")
    w_hi_ready = sem("w_hi_ready")
    w_lo_ready = sem("w_lo_ready")
    projected = sem("projected")
    plain_stored = sem("plain_stored")
    stack_hi = sem("stack_hi")
    stack_lo = sem("stack_lo")
    tanh_done = sem("tanh_done")
    gate_done = sem("gate_done")
    gated = sem("gated")
    b_scored = sem("b_scored")
    b_biased = sem("b_biased")
    b_exped = sem("b_exped")
    b_inverted = sem("b_inverted")
    b_ratio = sem("b_ratio")
    b_mixed = sem("b_mixed")
    b_valued = sem("b_valued")
    b_squared = sem("b_squared")
    b_meaned = sem("b_meaned")
    b_rooted = sem("b_rooted")
    b_scaled = sem("b_scaled")
    turned_full = sem("turned_full")
    turned_read = sem("turned_read")
    mixed_read = sem("mixed_read")
    a_scored = sem("a_scored")
    a_biased = sem("a_biased")
    a_sinked = sem("a_sinked")
    a_exped = sem("a_exped")
    a_summed = sem("a_summed")
    a_inverted = sem("a_inverted")
    a_weighted = sem("a_weighted")
    a_valued = sem("a_valued")
    wo_hi_ready = sem("wo_hi_ready")
    wo_lo_ready = [sem("wo_lo_ready0"), sem("wo_lo_ready1")]
    y_hi_ready = sem("y_hi_ready")
    y_lo_ready = sem("y_lo_ready")
    out_projected = sem("out_projected")
    y_squared = sem("y_squared")
    y_meaned = sem("y_meaned")
    y_rooted = sem("y_rooted")
    y_weighted = sem("y_weighted")
    y_added = sem("y_added")

    def x_turned_at(t):
        return scores[:, 1024 * (t % 2):1024 * (t % 2) + 1024].rearrange("p (k c) -> p k c", c=P)

    def by_chunk(tokens):
        return tokens.rearrange("p (c q) -> p c q", q=CHUNK)

    def a_half(j, half):
        return qT_A[:, j // 2, half * CHUNKS // 2:(half + 1) * CHUNKS // 2, j % 2, :]

    def a_scores_at(c, j):
        return 1024 * (c % 2) + 512 * (j // 2) + P * (j % 2)

    def y_parts(t, to):
        tokens = slice(P * t, P * t + P)
        a_parts = [(to[:, 2 * r:2 * r + 2, tokens].rearrange("p s (c q) -> p s c q", q=CHUNK),
                    qT_A[:, r, 2 * t:2 * t + 2].rearrange("p c s q -> p s c q")) for r in range(2)]
        return a_parts + [(to[:, A_PAIRS:KT, tokens], out_B[:, :, tokens])]

    def feature_parts(t):
        return [slice(0, KT // 2), slice(KT // 2, KT)] if t == 0 else [slice(0, KT)]

    def tile_count(t, part=None):
        return t + 2 if t or part is None else part + 1

    def halves_done(kind, index, half):
        return 2 * UNITS.index((kind, index)) + half + 1

    def plain_count(kind, index, half):
        return 2 * PLAIN.index(UNITS.index((kind, index))) + half + 1

    def stack_count(n, half):
        parts = [2 if UNITS[m][0] == "qB" else 4 for m in STACKED]
        at = STACKED.index(n)
        return 2 * sum(parts[:at]) + parts[at] * (half + 1)

    turned_users = [s for s in SCHEDULE
                    if s[0] in ("b_transpose", "b_finish_transpose", "a_transpose")]

    def turned_count(*step):
        return turned_users.index(step) + 1

    mixed_users = [s for s in SCHEDULE if s[0] == "a_values" or s[0] == "b_values" and s[1] % 4 == 3]

    def mixed_before(step):
        at = SCHEDULE.index(step)
        return sum(SCHEDULE.index(s) < at for s in mixed_users)

    def mixed_parts(u, r):
        parts = [1 + (v % TILES >= TILES // 2) for v in range(u + 1)]
        return sum(parts[:u]) + min(r + 1, parts[u])

    def gate_count(n, half):
        return 2 * GATES.index(n) + half + 1

    def proj_user(n, half):
        return 2 * TILES + 2 * n + half

    def wait_proj_free(engine, filling):
        before = filling - 2
        if before < 0:
            return
        if before < 2 * TILES:
            engine.wait_ge(v_stored, before + 1)
            return
        n, half = divmod(before - 2 * TILES, 2)
        if n in GATES:
            engine.wait_ge(gate_done, gate_count(n, half))
        elif n in STACKED:
            engine.wait_ge(stack_lo, stack_count(n, half))
        else:
            engine.wait_ge(plain_stored, plain_count(*UNITS[n], half))

    w_cols = w_in[0].rearrange("(k p) e -> p k e", p=P)

    def unit_columns(n):
        kind, i = UNITS[n]
        if kind == "kA":
            return [(AK, P)]
        if kind in ("qA", "gA"):
            first = (AQ if kind == "qA" else AG) + HEAD_DIM * i
            return [(first, HEAD_DIM), (first + A_PAIRS * HEAD_DIM, HEAD_DIM)]
        return [({"qB": BQ, "kB": BK, "gB": BG}[kind] + P * i, P)]

    def out_rows(k):
        if k < A_PAIRS:
            return [(HEAD_DIM * k, HEAD_DIM), (HEAD_DIM * (k + A_PAIRS), HEAD_DIM)]
        return [(A_WIDTH + P * B_ORDER[k - A_PAIRS], P)]

    def load_count(n):
        return sum(16 * len(unit_columns(m)) for m in range(n % RAW, n + 1, RAW))

    def wo_load_count(k):
        return sum(16 * len(out_rows(m)) for m in range(k % WO_RAW, k + 1, WO_RAW))

    def wo_raw(k):
        slot = k % WO_RAW
        if slot < 2:
            return wo_early[:, OLDEST + SPLIT * slot, :]
        return w_raw[:, slot - 2].rearrange("p k c -> p (k c)")

    v_runs = [[(BV, VG, 0)], [(BV + VG, B_WIDTH - VG, VG), (AV, P, B_WIDTH)]]

    with nc.Block() as block:

        @block.sync
        def _(sp):
            def load_x(t):
                if t >= XS:
                    sp.wait_ge(x_turned, tile_count(t - XS))
                sp.dma_start(x_in[:, t % XS, :], x[0, t * P:(t + 1) * P, :]).then_inc(x_loaded[t % XS], 16)

            load_x(0)
            sp.dma_start(pre_g[:, :], pre_norm_g[0:1, :].to_broadcast([P, D_MODEL])).then_inc(pre_g_loaded, 16)
            for part in range(2):
                k = slice(4 * part, 4 * part + 4)
                sp.dma_start(wv_raw[:, k, 0:VG], w_cols[:, k, BV:BV + VG]).then_inc(wv_loaded[part], 16)
            load_x(1)
            load_x(2)
            for i, (first, count, to) in enumerate(v_runs[1]):
                sp.dma_start(wv_raw[:, :, to:to + count],
                             w_cols[:, :, first:first + count]).then_inc(wv_loaded[2 + i], 16)
                load_x(3 + i)
            def load_small():
                sp.dma_start(sink_in, sinks[0:1, :].to_broadcast([P, A_HEADS])).then_inc(small_loaded, 16)
                sp.dma_start(sub_g, subln_g.rearrange("a e -> e a")).then_inc(small_loaded, 16)
                for v, vector in enumerate((lambda_q1, lambda_k1, lambda_q2, lambda_k2)):
                    sp.dma_start(lam_in[:, v, 0:HEAD_DIM],
                                 vector[0:1, :].to_broadcast([P, HEAD_DIM])).then_inc(small_loaded, 16)

            def load_w(n):
                if n >= RAW:
                    sp.wait_ge(w_hi_ready, n - RAW + 1)
                    sp.wait_ge(w_lo_ready, n - RAW + 1)
                to = 0
                for first, count in unit_columns(n):
                    sp.dma_start(w_raw[:, n % RAW, :, to:to + count],
                                 w_cols[:, :, first:first + count]).then_inc(w_loaded[n % RAW], 16)
                    to += count

            def load_wo(k):
                if k < 2:
                    sp.wait_ge(projected, 2 * (NU - SPLIT) + 2)
                elif k < WO_RAW:
                    sp.wait_ge(w_hi_ready, NU)
                    sp.wait_ge(w_lo_ready, NU)
                else:
                    sp.wait_ge(wo_hi_ready, k - WO_RAW + 1)
                    sp.wait_ge(wo_lo_ready[k % 2], (k - WO_RAW) // 2 + 1)
                to = 0
                for first, count in out_rows(k):
                    sp.dma_start(wo_raw(k)[to:to + count, :],
                                 w_out[0, first:first + count, :]).then_inc(wo_loaded[k % WO_RAW], 16)
                    to += count

            for t in range(5, TILES):
                load_x(t)
                if t < 7:
                    load_w(t - 5)
                if t == 5:
                    load_small()
            sp.wait_ge(pads_made, 1)
            sp.wait_ge(v_stored, 2 * TILES)
            a_cols = slice(B_WIDTH, V_WIDTH)
            sp.dma_start(v_shift[CHUNK:P, :, :], v_sb[0:CHUNK, :, a_cols]).then_inc(v_shifted, 16)
            sp.dma_start(v_shift[0:CHUNK, 1:TILES, :],
                         v_sb[CHUNK:P, 0:TILES - 1, a_cols]).then_inc(v_shifted, 16)
            for n in range(2, NU):
                load_w(n)
            for k in range(KT):
                load_wo(k)
            sp.wait_ge(projected, 2 * NU)
            sp.wait_ge(gated, 2 * len(GATES))
            sp.dma_start(post_g[:, :],
                         post_norm_g[0:1, :].to_broadcast([P, D_MODEL])).then_inc(post_g_loaded, 16)
            for t in range(TILES):
                if t >= 2:
                    sp.wait_ge(y_added, 2 * t - 2)
                sp.dma_start(x_res[:, t % 2, :], x[0, t * P:(t + 1) * P, :]).then_inc(res_loaded[t % 2], 16)
            for t in range(2):
                sp.wait_ge(stored[t], 16 * 2 * (TILES // 2))

        @block.gpsimd
        def _(pool):
            def low_weights(n):
                pool.wait_ge(w_hi_ready, n + 1)
                nc.gpsimd.tensor_tensor(w_lo[:, n % SPLIT], w_raw[:, n % RAW],
                                        w_hi[:, n % SPLIT].bitcast(F32), ALU.subtract).then_inc(w_lo_ready, 1)

            def root(out_, in_, width, done):
                nc.gpsimd.tensor_tensor(out_, in_, neg_half[:, 0:width], ALU.pow).then_inc(done, 1)

            nc.gpsimd.memset(neg_half, -0.5).then_inc(half_made, 1)
            nc.gpsimd.memset(ident[:, :], 0.0).then_inc(ident_made, 1)
            pool.wait_ge(ident_made, 1)
            nc.gpsimd.affine_select(out=ident[:, :], in_=ident[:, :], compare_op=ALU.not_equal, fill=1.0,
                                    base=0, pattern=[[-1, P]], channel_multiplier=1).then_inc(ident_made, 1)
            pool.wait_ge(half_made, 1)
            for t in range(TILES):
                pool.wait_ge(x_squared, t + 1)
                nc.gpsimd.tensor_scalar(x_mean[:, t:t + 1], x_square[:, t:t + 1], 1.0, EPS, ALU.mult,
                                        ALU.add).then_inc(x_meaned, 1)
                pool.wait_ge(x_meaned, t + 1)
                root(x_scale[:, t:t + 1], x_mean[:, t:t + 1], 1, x_scaled)
                if t == 0:
                    pool.wait_ge(wv_hi_ready, 1)
                    k, cols = slice(0, 4), slice(0, VG)
                    nc.gpsimd.tensor_tensor(wv_lo[:, k, cols], wv_raw[:, k, cols], wv_hi[:, k, cols].bitcast(F32),
                                            ALU.subtract).then_inc(wv_lo_first, 1)
                if t == 2:
                    nc.gpsimd.iota(dist_b[:, :], [[-1, SEQ]], base=SEQ - P, channel_multiplier=1,
                                   allow_small_or_imprecise_dtypes=True).then_inc(dist_made, 1)
                    nc.gpsimd.iota(dist_a[:, 1, :], [[-1, P]], base=CHUNK, channel_multiplier=1,
                                   allow_small_or_imprecise_dtypes=True).then_inc(dist_made, 1)
                if t == TILES - 1:
                    for n in (0, 1):
                        low_weights(n)
            for step, *i in SCHEDULE:
                if step == "split" and i[0] >= 2:
                    low_weights(i[0])
                elif step == "split_out" and i[0] % 2 == 0:
                    k = i[0]
                    pool.wait_ge(wo_hi_ready, k + 1)
                    nc.gpsimd.tensor_tensor(wo_lo[:, k, :], wo_raw(k), wo_hi[:, k, :].bitcast(F32),
                                            ALU.subtract).then_inc(wo_lo_ready[0], 1)
                elif step == "b_square":
                    f = i[0]
                    pool.wait_ge(b_squared, 4 * f + 4)
                    nc.gpsimd.tensor_scalar(mean_b, square_b, 1.0 / P, EPS, ALU.mult,
                                            ALU.add).then_inc(b_meaned, 1)
                    pool.wait_ge(b_meaned, f + 1)
                    if f:
                        pool.wait_ge(b_scaled, f)
                    root(rms_b, mean_b, 4, b_rooted)
                elif step == "a_weights":
                    c = i[0]
                    pool.wait_ge(a_inverted, c + 1)
                    w = a_weights[:, c % 2]
                    r = inv_a[:, 4 * (c % 2):4 * (c % 2) + 4].unsqueeze(2).to_broadcast([P, A_PAIRS, P])
                    nc.gpsimd.tensor_tensor(w, w, r, ALU.mult).then_inc(a_weighted, 1)
                elif step == "post":
                    t = i[0]
                    pool.wait_ge(y_meaned, t + 1)
                    root(y_scale[:, t % 2:t % 2 + 1], y_mean[:, t % 2:t % 2 + 1], 1, y_rooted)

        @block.scalar
        def _(act):
            def high_wv(k, cols, ready):
                act.wait_ge(wv_loaded[ready], 16)
                nc.scalar.activation(wv_hi[:, k, cols], wv_raw[:, k, cols], ACT.Copy).then_inc(wv_hi_ready, 1)

            def high_h(t, part=0):
                k = feature_parts(t)[part]
                act.wait_ge(x_turned, tile_count(t, part))
                nc.scalar.activation(hT_hi[:, k, t * P:(t + 1) * P], x_turned_at(t)[:, k],
                                     ACT.Copy).then_inc(h_hi_ready, 1)

            def square_x(t):
                act.wait_ge(x_loaded[t % XS], 16 * (t // XS + 1))
                if t:
                    act.wait_ge(x_squared, t)
                nc.scalar.activation(banks[:, :], x_in[:, t % XS, :], ACT.Square, scale=D_MODEL ** -0.5,
                                     accum_out=x_square[:, t:t + 1]).then_inc(x_squared, 1)

            def store_v(t, g):
                n = TILES * g + t
                act.wait_ge(v_projected, n + 1)
                nc.scalar.activation(v_sb[:, t, VG * g:VG * (g + 1)], proj[:, n % 2, 0:VG],
                                     ACT.Copy).then_inc(v_stored, 1)

            def high_weights(n):
                act.wait_ge(w_loaded[n % RAW], load_count(n))
                if n >= SPLIT:
                    act.wait_ge(projected, 2 * (n - SPLIT) + 2)
                nc.scalar.activation(w_hi[:, n % SPLIT], w_raw[:, n % RAW], ACT.Copy).then_inc(w_hi_ready, 1)

            square_x(0)
            high_h(0, 0)
            high_wv(slice(0, 4), slice(0, VG), 0)
            high_h(0, 1)
            high_wv(slice(4, 8), slice(0, VG), 1)
            square_x(1)
            for t in range(TILES):
                if t + 2 < TILES:
                    square_x(t + 2)
                if t + 1 < TILES:
                    high_h(t + 1)
                store_v(t, 0)
                if t == WV_AT:
                    high_wv(slice(0, 8), slice(VG, B_WIDTH), 2)
                if t == WV_AT + 1:
                    high_wv(slice(0, 8), slice(B_WIDTH, V_WIDTH), 3)
            for t in range(TILES):
                store_v(t, 1)
                if t < 2:
                    high_weights(t)
                if t == 4:
                    act.wait_ge(consts_made, 2)
                    nc.scalar.activation(lam_exp, lam_dot, ACT.Exp).then_inc(lam_exped, 1)

            for step, *i in SCHEDULE:
                if step == "split" and i[0] >= 2:
                    high_weights(i[0])
                elif step == "split_out":
                    k = i[0]
                    act.wait_ge(wo_loaded[k % WO_RAW], wo_load_count(k))
                    act.wait_ge(turned_full, len(turned_users))
                    nc.scalar.activation(wo_hi[:, k, :], wo_raw(k), ACT.Copy).then_inc(wo_hi_ready, 1)
                elif step == "store":
                    n, half = i
                    kind, head = UNITS[n]
                    source = proj[:, proj_user(n, half) % 2, :]
                    tokens = slice(HALF * half, HALF * half + HALF)
                    act.wait_ge(projected, 2 * n + half + 1)
                    if kind == "qB":
                        for m in range(2):
                            own = slice(HEAD_DIM * m, HEAD_DIM * (m + 1))
                            nc.scalar.activation(q_stack[head][m][own, tokens], source[own, :], ACT.Copy,
                                                 scale=SCALE / slope_b(head)).then_inc(stack_hi, 1)
                    elif kind == "kB":
                        if head:
                            act.wait_ge(b_scored, 2 * TILES * head)
                        for m in range(2):
                            own = slice(HEAD_DIM * m, HEAD_DIM * (m + 1))
                            for part in (own, slice(HEAD_DIM * (1 - m), HEAD_DIM * (2 - m))):
                                nc.scalar.activation(k_hi[part, m, tokens], source[own, :],
                                                     ACT.Copy).then_inc(stack_hi, 1)
                    elif kind == "kA":
                        to = kT_A[:, CHUNK + HALF * half:CHUNK + HALF * half + HALF]
                        nc.scalar.activation(to, source, ACT.Copy).then_inc(plain_stored, 1)
                    elif kind == "qA":
                        act.wait_ge(slopes_made, 4 * A_PAIRS)
                        nc.scalar.activation(a_half(head, half), by_chunk(source), ACT.Copy,
                                             scale=q_scale[:, head:head + 1]).then_inc(plain_stored, 1)
                    else:
                        g = gate_count(n, half) - 1
                        if g:
                            act.wait_ge(gated, g)
                        nc.scalar.activation(gate[:, :], source, ACT.Tanh, scale=0.5).then_inc(tanh_done, 1)
                elif step == "b_exp":
                    u = i[0]
                    keys = P * (u % TILES + 1)
                    for m in range(2):
                        w = weights_1[:, 0:keys] if m else weights_0[:, u % 2, 0:keys]
                        act.wait_ge(b_biased, 2 * u + m + 1)
                        nc.scalar.activation(w, w, ACT.Exp, scale=-1.0, bias=min_b[:, 2 * u + m:2 * u + m + 1],
                                             accum_out=sum_b[:, 2 * u + m:2 * u + m + 1]).then_inc(b_exped, 1)
                elif step == "b_transpose":
                    u, r = i
                    blocks = min(4, u % TILES + 1 - 4 * r)
                    if u:
                        act.wait_ge(b_valued, u)
                    if u == 3 * TILES:
                        act.wait_ge(a_valued, CHUNKS)
                    act.wait_ge(turned_full, turned_count("b_transpose", u, r))
                    nc.scalar.activation(weightsT[:, 4 * r:4 * r + blocks, :],
                                         turned[:, 0:P * blocks].rearrange("p (b q) -> p b q", q=P),
                                         ACT.Copy).then_inc(turned_read, 1)
                elif step == "b_square":
                    f = i[0]
                    act.wait_ge(b_valued, 4 * f + 4)
                    if f:
                        act.wait_ge(b_meaned, f)
                    for j in range(4):
                        u = 4 * f + j
                        if 4 * f + j:
                            act.wait_ge(b_squared, 4 * f + j)
                        nc.scalar.activation(junk[:, :], mixed[:, P * j:P * j + P], ACT.Square,
                                             scale=inv_b[:, 2 * u:2 * u + 1],
                                             accum_out=square_b[:, j:j + 1]).then_inc(b_squared, 1)
                elif step == "b_finish_transpose":
                    f = i[0]
                    act.wait_ge(turned_full, turned_count("b_finish_transpose", f))
                    act.wait_ge(consts_made, 5)
                    tokens = slice(HALF * (f % 2), HALF * (f % 2) + HALF)
                    nc.scalar.activation(out_B[:, B_ORDER.index(f // 2), tokens], turned[:, :],
                                         ACT.Copy, scale=out_g).then_inc(turned_read, 1)
                elif step == "a_scores":
                    c = i[0]
                    s = 4 * (c % 2)
                    for j in range(A_PAIRS):
                        w = a_weights[:, c % 2, j, :]
                        act.wait_ge(a_biased, 4 * c + j + 1)
                        nc.scalar.activation(w, w, ACT.Exp, scale=-1.0, bias=min_a[:, s + j:s + j + 1],
                                             accum_out=sum_a[:, s + j:s + j + 1]).then_inc(a_exped, 1)
                    act.wait_ge(a_sinked, c + 1)
                    nc.scalar.activation(sink_w[:, s:s + 4], sink_arg[:, s:s + 4], ACT.Exp).then_inc(a_exped, 1)
                elif step == "a_transpose":
                    c = i[0]
                    if c:
                        act.wait_ge(a_valued, c)
                    else:
                        act.wait_ge(b_valued, 3 * TILES)
                    act.wait_ge(turned_full, turned_count("a_transpose", c))
                    nc.scalar.activation(a_weightsT[:, :, :], turned[:, :].rearrange("p (j q) -> p j q", q=P),
                                         ACT.Copy).then_inc(turned_read, 1)
                elif step == "y_split":
                    t = i[0]
                    tokens = slice(P * t, P * t + P)
                    half = t // 4
                    act.wait_ge(projected, 2 * NU - 1 + half)
                    act.wait_ge(gated, 2 * len(GATES) - 1 + half)
                    for to, part in y_parts(t, hT_hi):
                        nc.scalar.activation(to, part, ACT.Copy).then_inc(y_hi_ready, 1)
                elif step == "out_project":
                    t, half = i
                    act.wait_ge(out_projected, 2 * t + half + 1)
                    if t >= 2:
                        act.wait_ge(y_meaned, t - 1)
                    if 2 * t + half:
                        act.wait_ge(y_squared, 2 * t + half)
                    at = 1024 * (t % 2) + HALF * half
                    s = 2 * (t % 2) + half
                    nc.scalar.activation(turned, scores[:, at:at + HALF], ACT.Square, scale=D_MODEL ** -0.5,
                                         accum_out=y_square[:, s:s + 1]).then_inc(y_squared, 1)
                elif step == "post":
                    t = i[0]
                    for half in range(2):
                        act.wait_ge(y_added, 2 * t + half + 1)
                        cols = slice(HALF * half, HALF * half + HALF)
                        act.dma_start(out[0, P * t:P * t + P, cols],
                                      y_out[:, t % 2, cols]).then_inc(stored[t % 2], 16)

        @block.vector
        def _(dve):
            def norm_x(t):
                if t == 0:
                    dve.wait_ge(pre_g_loaded, 16)
                dve.wait_ge(x_scaled, t + 1)
                for k in feature_parts(t):
                    cols = slice(P * k.start, P * k.stop)
                    nc.vector.scalar_tensor_tensor(x_in[:, t % XS, cols], x_in[:, t % XS, cols],
                                                   x_scale[:, t:t + 1], pre_g[:, cols], ALU.mult,
                                                   ALU.mult).then_inc(x_normed, 1)

            def low_h(t):
                tokens = slice(P * t, P * t + P)
                for part, k in enumerate(feature_parts(t)):
                    dve.wait_ge(h_hi_ready, tile_count(t, part))
                    nc.vector.tensor_tensor(hT_lo[:, k, tokens], x_turned_at(t)[:, k],
                                            hT_hi[:, k, tokens].bitcast(F32), ALU.subtract).then_inc(h_lo_ready, 1)

            def low_wv(k, cols, part):
                dve.wait_ge(wv_hi_ready, part + 1)
                nc.vector.tensor_tensor(wv_lo[:, k, cols], wv_raw[:, k, cols], wv_hi[:, k, cols].bitcast(F32),
                                        ALU.subtract).then_inc(wv_lo_ready, 1)

            def constants():
                dve.wait_ge(small_loaded, 16 * 6)
                for d in range(2):
                    a, b = (lam_in[:, v, 0:HEAD_DIM] for v in (2 * d, 2 * d + 1))
                    nc.vector.tensor_tensor_reduce(out=junk[:, HEAD_DIM * d:HEAD_DIM * (d + 1)], in0=a, in1=b,
                                                   scale=1.0, scalar=0.0, op0=ALU.mult, op1=ALU.add,
                                                   accum_out=lam_dot[:, d:d + 1]).then_inc(consts_made, 1)
                for side, part in enumerate((slice(0, CHUNK), slice(CHUNK, P))):
                    nc.vector.tensor_scalar(neg_sink[part, :], sink_in[part, side::2], -1.0, None,
                                            ALU.mult).then_inc(consts_made, 1)
                nc.vector.tensor_scalar(out_g, sub_g, 0.5 * (1.0 - LAMBDA_INIT), None,
                                        ALU.mult).then_inc(consts_made, 1)
                for j in range(A_PAIRS):
                    for side, part in enumerate((slice(0, CHUNK), slice(CHUNK, P))):
                        nc.vector.memset(q_scale[part, j:j + 1],
                                         SCALE / slope_a(j + A_PAIRS * side)).then_inc(slopes_made, 1)
                        nc.vector.memset(neg_slope[part, j:j + 1], -slope_a(2 * j + side)).then_inc(slopes_made, 1)
                nc.vector.memset(v_shift[0:CHUNK, 0, :], 0.0).then_inc(pads_made, 1)
                dve.wait_ge(dist_made, 2)
                lower = dist_a[CHUNK:P, 1, :]
                nc.vector.tensor_scalar(lower, lower, float(CHUNK), None, ALU.subtract).then_inc(dist_ready, 1)
                dve.wait_ge(dist_ready, 1)
                for d in (dist_b[:, :], dist_a[:, 1, :]):
                    nc.vector.scalar_tensor_tensor(d, d, -1.0, d, ALU.mult, ALU.min).then_inc(dist_ready, 1)
                dve.wait_ge(dist_ready, 3)
                nc.vector.memset(dist_b[0:CHUNK, SEQ - CHUNK:SEQ], MASKED).then_inc(dist_ready, 1)
                nc.vector.tensor_copy(dist_a[:, 0, CHUNK:P], dist_a[:, 1, CHUNK:P]).then_inc(dist_ready, 1)
                nc.vector.memset(dist_a[:, 0, 0:CHUNK], MASKED).then_inc(dist_ready, 1)

            def make_lambda():
                dve.wait_ge(lam_exped, 1)
                nc.vector.tensor_tensor(lam_dif, lam_exp[:, 1:2], lam_exp[:, 0:1],
                                        ALU.subtract).then_inc(consts_made, 1)
                dve.wait_ge(consts_made, 6)
                nc.vector.tensor_scalar(neg_lam, lam_dif, LAMBDA_INIT, None, ALU.subtract).then_inc(consts_made, 1)

            norm_x(0)
            low_h(0)
            low_wv(slice(4, 8), slice(0, VG), 1)
            norm_x(1)
            for t in range(TILES):
                if t + 2 < TILES:
                    norm_x(t + 2)
                if t + 1 < TILES:
                    low_h(t + 1)
                if t == WV_AT:
                    low_wv(slice(0, 8), slice(VG, B_WIDTH), 2)
                if t == WV_AT + 1:
                    low_wv(slice(0, 8), slice(B_WIDTH, V_WIDTH), 3)
            constants()
            make_lambda()
            dve.wait_ge(v_projected, 2 * TILES)
            nc.vector.memset(kT_A[:, 0:CHUNK], 0.0).then_inc(pads_made, 1)
            dve.wait_ge(dist_ready, 6)

            for step, *i in SCHEDULE:
                if step == "store_low":
                    n, half = i
                    kind, head = UNITS[n]
                    source = proj[:, proj_user(n, half) % 2, :]
                    tokens = slice(HALF * half, HALF * half + HALF)
                    dve.wait_ge(stack_hi, stack_count(n, half))
                    for m in range(2):
                        own = slice(HEAD_DIM * m, HEAD_DIM * (m + 1))
                        other = slice(HEAD_DIM * (1 - m), HEAD_DIM * (2 - m))
                        if kind == "qB":
                            q = q_stack[head][m]
                            nc.vector.scalar_tensor_tensor(
                                q[other, tokens], source[own, :], SCALE / slope_b(head), q[own, tokens].bitcast(F32),
                                ALU.mult, ALU.subtract).then_inc(stack_lo, 1)
                        else:
                            for part in (own, other):
                                nc.vector.tensor_tensor(k_lo[part, m, tokens], source[own, :],
                                                        k_hi[own, m, tokens].bitcast(F32),
                                                        ALU.subtract).then_inc(stack_lo, 1)
                elif step == "gate":
                    n, half = i
                    kind, head = UNITS[n]
                    g = gate_count(n, half) - 1
                    tokens = slice(HALF * half, HALF * half + HALF)
                    source = proj[:, proj_user(n, half) % 2, :]
                    o = by_chunk(out_B[:, B_ORDER.index(head), tokens]) if kind == "gB" else a_half(head, half)
                    dve.wait_ge(tanh_done, g + 1)
                    nc.vector.scalar_tensor_tensor(gate[:, :], gate[:, :], 1.0, source,
                                                   ALU.add, ALU.mult).then_inc(gate_done, 1)
                    dve.wait_ge(gate_done, g + 1)
                    if kind == "gB":
                        dve.wait_ge(turned_read, turned_count("b_finish_transpose", 2 * head + half))
                    else:
                        dve.wait_ge(mixed_read, mixed_users.index(("a_values", CHUNKS - 1)) + 1)
                    nc.vector.tensor_tensor(o, by_chunk(gate[:, :]), o, ALU.mult).then_inc(gated, 1)
                elif step == "split_out" and i[0] % 2 == 1:
                    k = i[0]
                    dve.wait_ge(wo_hi_ready, k + 1)
                    nc.vector.tensor_tensor(wo_lo[:, k, :], wo_raw(k), wo_hi[:, k, :].bitcast(F32),
                                            ALU.subtract).then_inc(wo_lo_ready[1], 1)
                elif step == "b_mix":
                    u = i[0]
                    keys = P * (u % TILES + 1)
                    dve.wait_ge(b_exped, 2 * u + 2)
                    pair = slice(2 * u, 2 * u + 2)
                    nc.vector.reciprocal(inv_b[:, pair], sum_b[:, pair]).then_inc(b_inverted, 1)
                    dve.wait_ge(b_inverted, u + 1)
                    nc.vector.tensor_scalar(mix_b[:, u:u + 1], sum_b[:, 2 * u:2 * u + 1],
                                            inv_b[:, 2 * u + 1:2 * u + 2], neg_lam, ALU.mult,
                                            ALU.mult).then_inc(b_ratio, 1)
                    dve.wait_ge(b_ratio, u + 1)
                    for first in range(0, keys, HALF):
                        part = slice(first, min(first + HALF, keys))
                        w0, w1 = weights_0[:, u % 2, part], weights_1[:, part]
                        nc.vector.scalar_tensor_tensor(w0, w1, mix_b[:, u:u + 1], w0, ALU.mult,
                                                       ALU.add).then_inc(b_mixed, 1)
                elif step == "b_scores":
                    u = i[0]
                    keys = P * (u % TILES + 1)
                    if u >= 2:
                        dve.wait_ge(turned_full, turned_count("b_transpose", u - 2, ((u - 2) % TILES) // 4))
                    if u:
                        dve.wait_ge(b_mixed, mixed_parts(u - 1, 1))
                    if u == 3 * TILES:
                        dve.wait_ge(turned_full, turned_count("a_transpose", CHUNKS - 2))
                    if u == 3 * TILES + 2:
                        dve.wait_ge(turned_full, turned_count("a_transpose", CHUNKS - 1))
                    for m in range(2):
                        dve.wait_ge(b_scored, 2 * u + m + 1)
                        nc.vector.tensor_tensor_reduce(
                            out=weights_1[:, 0:keys] if m else weights_0[:, u % 2, 0:keys],
                            in0=scores[:, 1024 * m:1024 * m + keys],
                            in1=dist_b[:, SEQ - keys:SEQ], scale=-slope_b(u // TILES), scalar=-MASKED,
                            op0=ALU.add, op1=ALU.min,
                            accum_out=min_b[:, 2 * u + m:2 * u + m + 1]).then_inc(b_biased, 1)
                elif step == "b_finish":
                    f = i[0]
                    dve.wait_ge(b_rooted, f + 1)
                    inv_0 = inv_b[:, 8 * f:8 * f + 8].rearrange("p (u m) -> p u m", m=2)[:, :, 0]
                    nc.vector.tensor_tensor(scale_b, rms_b, inv_0, ALU.mult).then_inc(b_scaled, 1)
                    dve.wait_ge(b_scaled, f + 1)
                    if f:
                        dve.wait_ge(turned_full, turned_count("b_finish_transpose", f - 1))
                    nc.vector.tensor_tensor(on_b[:, :, :], mixed.rearrange("p (u e) -> p u e", e=P),
                                            scale_b.unsqueeze(2).to_broadcast([P, 4, P]),
                                            ALU.mult).then_inc(mixed_read, 1)
                elif step == "a_scores":
                    c = i[0]
                    s = 4 * (c % 2)
                    if c == 0:
                        dve.wait_ge(slopes_made, 4 * A_PAIRS)
                        dve.wait_ge(b_mixed, mixed_parts(3 * TILES - 1, 1))
                    if c >= 2:
                        dve.wait_ge(turned_full, turned_count("a_transpose", c - 2))
                    dve.wait_ge(a_scored, c + 1)
                    for j in range(A_PAIRS):
                        nc.vector.tensor_tensor_reduce(
                            out=a_weights[:, c % 2, j, :], in0=scores[:, a_scores_at(c, j):a_scores_at(c, j) + P],
                            in1=dist_a[:, min(c, 1), :], scale=neg_slope[:, j:j + 1], scalar=neg_sink[:, j:j + 1],
                            op0=ALU.add, op1=ALU.min, accum_out=min_a[:, s + j:s + j + 1]).then_inc(a_biased, 1)
                    dve.wait_ge(a_biased, 4 * c + 4)
                    nc.vector.tensor_tensor(sink_arg[:, s:s + 4], min_a[:, s:s + 4], neg_sink,
                                            ALU.subtract).then_inc(a_sinked, 1)
                elif step == "a_weights":
                    c = i[0]
                    s = 4 * (c % 2)
                    dve.wait_ge(a_exped, 5 * c + 5)
                    nc.vector.tensor_tensor(total_a[:, s:s + 4], sum_a[:, s:s + 4], sink_w[:, s:s + 4],
                                            ALU.add).then_inc(a_summed, 1)
                    dve.wait_ge(a_summed, c + 1)
                    nc.vector.reciprocal(inv_a[:, s:s + 4], total_a[:, s:s + 4]).then_inc(a_inverted, 1)
                elif step == "a_values":
                    c = i[0]
                    dve.wait_ge(a_valued, c + 1)
                    nc.vector.tensor_scalar(qT_A[:, :, c],
                                            mixed[:, 0:A_PAIRS * CHUNK].rearrange("p (r s q) -> p r s q", s=2, q=CHUNK),
                                            0.5, None, ALU.mult).then_inc(mixed_read, 1)
                elif step == "y_split":
                    t = i[0]
                    tokens = slice(P * t, P * t + P)
                    for p, ((to, part), (high, _)) in enumerate(zip(y_parts(t, hT_lo), y_parts(t, hT_hi))):
                        dve.wait_ge(y_hi_ready, Y_PARTS * t + p + 1)
                        nc.vector.tensor_tensor(to, part, high.bitcast(F32), ALU.subtract).then_inc(y_lo_ready, 1)
                elif step == "post":
                    t = i[0]
                    if t == 0:
                        dve.wait_ge(post_g_loaded, 16)
                    if t >= 2:
                        dve.wait_ge(stored[t % 2], 32 * (t // 2))
                    s = 2 * (t % 2)
                    for half in range(2):
                        cols = slice(HALF * half, HALF * half + HALF)
                        at = 1024 * (t % 2) + HALF * half
                        dve.wait_ge(y_squared, 2 * t + half + 1)
                        if half:
                            nc.vector.scalar_tensor_tensor(
                                y_mean[:, t % 2:t % 2 + 1], y_square[:, s:s + 1], EPS, y_square[:, s + 1:s + 2],
                                ALU.add, ALU.add).then_inc(y_meaned, 1)
                        nc.vector.tensor_tensor(y_out[:, t % 2, cols], scores[:, at:at + HALF], post_g[:, cols],
                                                ALU.mult).then_inc(y_weighted, 1)
                    dve.wait_ge(y_weighted, 2 * t + 2)
                    dve.wait_ge(res_loaded[t % 2], 16 * (t // 2 + 1))
                    dve.wait_ge(y_rooted, t + 1)
                    for half in range(2):
                        cols = slice(HALF * half, HALF * half + HALF)
                        nc.vector.scalar_tensor_tensor(y_out[:, t % 2, cols], y_out[:, t % 2, cols],
                                                       y_scale[:, t % 2:t % 2 + 1], x_res[:, t % 2, cols],
                                                       ALU.mult, ALU.add).then_inc(y_added, 1)

        @block.tensor
        def _(pe):
            def turn_x(t):
                if t >= 2:
                    pe.wait_ge(h_lo_ready, tile_count(t - 2))
                for part, ks in enumerate(feature_parts(t)):
                    pe.wait_ge(x_normed, tile_count(t, part))
                    for k in range(ks.start, ks.stop):
                        at = 1024 * (t % 2) + P * k
                        last = nc.tensor.transpose(scores[:, at:at + P], x_in[:, t % XS, P * k:P * k + P],
                                                   ident[:, :])
                    last.then_inc(x_turned, 1)

            def project_v(t, g):
                n = TILES * g + t
                wait_proj_free(pe, n)
                pe.wait_ge(h_hi_ready, tile_count(t, 0))
                tokens, cols = slice(P * t, P * t + P), slice(VG * g, VG * (g + 1))
                for p, (h, w) in enumerate(((hT_hi, wv_hi), (hT_lo, wv_hi), (hT_hi, wv_lo))):
                    if p == 1:
                        pe.wait_ge(h_lo_ready, tile_count(t))
                    for k in range(KT):
                        if n == 0 and k % 4 == 0:
                            if p == 0 and k:
                                pe.wait_ge(h_hi_ready, tile_count(0))
                            if p < 2:
                                pe.wait_ge(wv_hi_ready, k // 4 + 1)
                            elif k == 0:
                                pe.wait_ge(wv_lo_first, 1)
                            else:
                                pe.wait_ge(wv_lo_ready, 1)
                        elif n == TILES and k == 0:
                            if p < 2:
                                pe.wait_ge(wv_hi_ready, 4)
                            else:
                                pe.wait_ge(wv_lo_ready, 3)
                        last = nc.tensor.matmul(proj[:, n % 2, 0:VG], h[:, k, tokens], w[:, k, cols],
                                                start=(p == 0 and k == 0), stop=(p == PASSES - 1 and k == KT - 1))
                last.then_inc(v_projected, 1)

            pe.wait_ge(ident_made, 2)
            for _ in range(WARM_UP):
                nc.tensor.transpose(proj[:, 1, 0:P], ident[:, :], ident[:, :])
            turn_x(0)
            for t in range(TILES):
                project_v(t, 0)
                if t == 0:
                    turn_x(1)
                if t + 2 < TILES:
                    turn_x(t + 2)
            for t in range(TILES):
                project_v(t, 1)

            for step, *i in SCHEDULE:
                if step == "project":
                    n, half, p = i
                    to = proj[:, proj_user(n, half) % 2, :]
                    slot = n % SPLIT
                    if p == 0:
                        wait_proj_free(pe, proj_user(n, half))
                        pe.wait_ge(w_hi_ready, n + 1)
                    which, first = divmod(p * KP, KT)
                    if which == PASSES - 1:
                        pe.wait_ge(w_lo_ready, n + 1)
                    w, h = ((w_hi, hT_hi), (w_hi, hT_lo), (w_lo, hT_hi))[which]
                    for k in range(first, first + KP):
                        last = nc.tensor.matmul(to, w[:, slot, k, :], h[:, k, HALF * half:HALF * half + HALF],
                                                start=(p == 0 and k == first),
                                                stop=(p == PIECES - 1 and k == KT - 1))
                    if p == PIECES - 1:
                        last.then_inc(projected, 1)
                elif step == "b_scores":
                    u = i[0]
                    head, block_ = divmod(u, TILES)
                    keys = P * (block_ + 1)
                    pe.wait_ge(stack_lo, max(stack_count(UNITS.index((kind, head)), block_ // 4)
                                             for kind in ("qB", "kB")))
                    if u == 3 * TILES:
                        pe.wait_ge(a_biased, A_PAIRS * CHUNKS)
                    for m in range(2):
                        if u:
                            pe.wait_ge(b_biased, 2 * u - 1 + m)
                        for first in range(0, keys, HALF):
                            width = min(HALF, keys - first)
                            for which, k in enumerate((k_hi, k_lo)):
                                last = nc.tensor.matmul(scores[:, 1024 * m + first:1024 * m + first + width],
                                                        q_stack[head][m][:, P * block_:P * block_ + P],
                                                        k[:, m, first:first + width],
                                                        start=(which == 0), stop=(which == 1))
                        last.then_inc(b_scored, 1)
                elif step == "b_transpose":
                    u, r = i
                    pe.wait_ge(b_mixed, mixed_parts(u, r))
                    if u or r:
                        pe.wait_ge(turned_read, turned_count("b_transpose", u, r) - 1)
                    for b in range(4 * r, min(4 * r + 4, u % TILES + 1)):
                        last = nc.tensor.transpose(turned[:, P * (b - 4 * r):P * (b - 4 * r) + P],
                                                   weights_0[:, u % 2, P * b:P * b + P], ident[:, :])
                    last.then_inc(turned_full, 1)
                elif step == "b_values":
                    u = i[0]
                    head, blocks = u // TILES, u % TILES + 1
                    pe.wait_ge(turned_read, turned_count("b_transpose", u, (blocks - 1) // 4))
                    if u % 4 == 0 and mixed_before((step, *i)):
                        pe.wait_ge(mixed_read, mixed_before((step, *i)))
                    for b in range(blocks):
                        last = nc.tensor.matmul(mixed[:, P * (u % 4):P * (u % 4) + P], weightsT[:, b, :],
                                                v_sb[:, b, P * head:P * head + P],
                                                start=(b == 0), stop=(b == blocks - 1))
                    last.then_inc(b_valued, 1)
                elif step == "b_finish_transpose":
                    f = i[0]
                    pe.wait_ge(mixed_read, mixed_users.index(("b_values", 4 * f + 3)) + 1)
                    pe.wait_ge(turned_read, turned_count(step, f) - 1)
                    for j in range(4):
                        last = nc.tensor.transpose(turned[:, P * j:P * j + P], on_b[:, j, :], ident[:, :])
                    last.then_inc(turned_full, 1)
                elif step == "a_scores":
                    c = i[0]
                    if c == 0:
                        pe.wait_ge(pads_made, 2)
                        pe.wait_ge(v_shifted, 32)
                        pe.wait_ge(plain_stored, plain_count("qA", A_PAIRS - 1, 1))
                        pe.wait_ge(b_biased, 2 * 3 * TILES)
                    if c >= 2:
                        pe.wait_ge(a_biased, A_PAIRS * (c - 1))
                    for j in range(A_PAIRS):
                        part = slice(HEAD_DIM * (j // 2), HEAD_DIM * (j // 2 + 1))
                        at = a_scores_at(c, j)
                        pair = qT_A[part, j % 2, c].rearrange("p s q -> p (s q)")
                        last = nc.tensor.matmul(scores[:, at:at + P], pair, kT_A[part, CHUNK * c:CHUNK * c + P],
                                                start=True, stop=True)
                    last.then_inc(a_scored, 1)
                elif step == "a_transpose":
                    c = i[0]
                    pe.wait_ge(a_weighted, c + 1)
                    pe.wait_ge(turned_read, turned_count(step, c) - 1)
                    for j in range(A_PAIRS):
                        last = nc.tensor.transpose(turned[:, P * j:P * j + P], a_weights[:, c % 2, j, :],
                                                   ident[:, :])
                    last.then_inc(turned_full, 1)
                elif step == "a_values":
                    c = i[0]
                    pe.wait_ge(turned_read, turned_count("a_transpose", c))
                    pe.wait_ge(mixed_read, mixed_before((step, *i)))
                    for h in range(2):
                        part = slice(HEAD_DIM * h, HEAD_DIM * (h + 1))
                        v = v_sb[:, c // 2, B_WIDTH:V_WIDTH] if c % 2 else v_shift[:, c // 2, :]
                        last = nc.tensor.matmul(mixed[part, 0:A_PAIRS * CHUNK], v[:, part],
                                                a_weightsT[:, 2 * h:2 * h + 2, :], start=True, stop=True)
                    last.then_inc(a_valued, 1)
                elif step == "out_project":
                    t, half = i
                    tokens, cols = slice(P * t, P * t + P), slice(HALF * half, HALF * half + HALF)
                    pe.wait_ge(y_lo_ready, Y_PARTS * (t + 1))
                    if t >= 2:
                        pe.wait_ge(y_weighted, 2 * (t - 2) + half + 1)
                    at = 1024 * (t % 2) + HALF * half
                    for p, (y, w) in enumerate(((hT_hi, wo_hi), (hT_lo, wo_hi), (hT_hi, wo_lo))):
                        for k in range(KT):
                            if t == 0 and half == 0 and p != 1:
                                if p:
                                    pe.wait_ge(wo_lo_ready[k % 2], k // 2 + 1)
                                else:
                                    pe.wait_ge(wo_hi_ready, k + 1)
                            last = nc.tensor.matmul(scores[:, at:at + HALF], y[:, k, tokens], w[:, k, cols],
                                                    start=(p == 0 and k == 0), stop=(p == PASSES - 1 and k == KT - 1))
                    last.then_inc(out_projected, 1)


INPUTS = ["x", "w_in", "w_out", "pre_norm_g", "post_norm_g", "sinks", "lambda_q1", "lambda_k1",
          "lambda_q2", "lambda_k2", "subln_g"]


def kernel(**inputs):
    import concourse.bacc as bacc
    import numpy as np
    from concourse.bass_utils import run_bass_kernel_spmd

    nc = bacc.Bacc("TRN2", target_bir_lowering=False, num_devices=1)
    arrays = {f"in_{name}": np.ascontiguousarray(inputs[name]) for name in INPUTS}
    args = [nc.dram_tensor(name, a.shape, mybir.dt.from_np(a.dtype), kind="ExternalInput").ap()
            for name, a in arrays.items()]
    out = nc.dram_tensor("out", (1, SEQ, D_MODEL), mybir.dt.float32, kind="ExternalOutput").ap()
    hybrid_layer(nc, *args, out)
    result = run_bass_kernel_spmd(nc, [arrays], core_ids=[0])
    return result.results[0]["out"]
```
